# Optimizing a Trainium2 kernel written in Bass

```python
import jax, jax.numpy as jnp
from jax import lax
import numpy as np

D_MODEL = 1024
BATCH = 1
SEQ = 1024
DEPTH = 1

CHUNK = 64
Q_BLOCK = 128
HEAD_DIM = 64
N_HEADS_A = 8
N_HEADS_B = 8
IDX_HEADS = 8
IDX_DIM = 64
TOPK_MAX = 256
ROPE_DIM = HEAD_DIM // 4
ROPE_THETA = 500000.0
N_GROUPS = 4
EXPERTS_PER_GROUP = 8
N_EXPERTS = N_GROUPS * EXPERTS_PER_GROUP
TOPK_IN_GROUP = 2
D_EXPERT = 512
EXPERT_BLOCK = 128
RMS_EPS = 1e-6
NEG_INF = -1e30
ATTN_SCALE = HEAD_DIM ** -0.5
IDX_SCALE = IDX_DIM ** -0.5

W_IN_SPLITS = (N_HEADS_A * HEAD_DIM, HEAD_DIM, HEAD_DIM, IDX_HEADS * IDX_DIM, IDX_DIM, IDX_HEADS,
               N_HEADS_B * HEAD_DIM, N_HEADS_B * HEAD_DIM, N_HEADS_B * HEAD_DIM, N_HEADS_B,
               D_MODEL, D_MODEL)
W_IN_COLS = sum(W_IN_SPLITS)

kernel_name = 'hybrid_dsa_fox_hiermoe_adaln_block'

def _split_cols(proj):
    offs = []
    acc = 0
    for w in W_IN_SPLITS[:-1]:
        acc += w
        offs.append(acc)
    return jnp.split(proj, offs, axis=-1)

def rmsnorm(t, g):
    tf = t.astype(jnp.float32)
    tf = tf * lax.rsqrt(jnp.mean(tf * tf, axis=-1, keepdims=True) + RMS_EPS)
    return (tf * g.astype(jnp.float32)).astype(t.dtype)

def modulate(h, shift, scale):
    return h * (1.0 + scale[:, None, :]) + shift[:, None, :]

def rope_tables(positions):
    inv_freq = ROPE_THETA ** (-jnp.arange(0, ROPE_DIM, 2, dtype=jnp.float32) / ROPE_DIM)
    ang = positions.astype(jnp.float32)[..., None] * inv_freq
    return jnp.cos(ang), jnp.sin(ang)

def partial_rope(t, cos, sin):
    extra = t.ndim - 3
    cos = cos.reshape(cos.shape[:2] + (1,) * extra + cos.shape[2:])
    sin = sin.reshape(sin.shape[:2] + (1,) * extra + sin.shape[2:])
    half = ROPE_DIM // 2
    r = t[..., :ROPE_DIM].astype(jnp.float32)
    r1, r2 = r[..., :half], r[..., half:]
    rot = jnp.concatenate([r1 * cos - r2 * sin, r2 * cos + r1 * sin], axis=-1)
    return jnp.concatenate([rot.astype(t.dtype), t[..., ROPE_DIM:]], axis=-1)

def token_mixers(h, cos, sin, w_in, b_forget, w_out_a, w_out_b, w_out):
    B, S, _ = h.shape
    nb = S // Q_BLOCK
    topk = min(TOPK_MAX, S // 4)
    qa, ka, va, qi, ki, wi, qb, kb, vb, fb, ga, gb = _split_cols(h @ w_in)

    qa = partial_rope(qa.reshape(B, S, N_HEADS_A, HEAD_DIM), cos, sin)
    ka = partial_rope(ka, cos, sin)
    qi = partial_rope(qi.reshape(B, S, IDX_HEADS, IDX_DIM), cos, sin)
    ki = partial_rope(ki, cos, sin)
    wi = wi * IDX_HEADS ** -0.5
    chunk_id = jnp.arange(S) // CHUNK

    def blocks(t):
        return jnp.swapaxes(t.reshape((B, nb, Q_BLOCK) + t.shape[2:]), 0, 1)

    def unblock(t):
        return jnp.swapaxes(t, 0, 1).reshape((B, S) + t.shape[3:])

    def dsa_block(args):
        bi, q_blk, qi_blk, wi_blk = args
        q_chunk = (bi * Q_BLOCK + jnp.arange(Q_BLOCK)) // CHUNK
        rel = jnp.einsum('bqhd,bsd->bqhs', qi_blk, ki,
                         preferred_element_type=jnp.float32) * IDX_SCALE
        score = jnp.einsum('bqh,bqhs->bqs', wi_blk.astype(jnp.float32), jax.nn.relu(rel))
        admissible = chunk_id[None, :] <= q_chunk[:, None]
        score = jnp.where(admissible[None], score, NEG_INF)
        _, sel = lax.top_k(score, topk)
        valid = chunk_id[sel] <= q_chunk[None, :, None]
        k_sel = jax.vmap(lambda t, i: t[i])(ka, sel)
        v_sel = jax.vmap(lambda t, i: t[i])(va, sel)
        logit = jnp.einsum('bqhd,bqkd->bqhk', q_blk, k_sel,
                           preferred_element_type=jnp.float32) * ATTN_SCALE
        logit = jnp.where(valid[:, :, None, :], logit, NEG_INF)
        p = jax.nn.softmax(logit, axis=-1).astype(v_sel.dtype)
        return jnp.einsum('bqhk,bqkd->bqhd', p, v_sel)

    oa = unblock(lax.map(dsa_block, (jnp.arange(nb), blocks(qa), blocks(qi), blocks(wi))))

    qb = qb.reshape(B, S, N_HEADS_B, HEAD_DIM)
    kb = kb.reshape(B, S, N_HEADS_B, HEAD_DIM)
    vb = vb.reshape(B, S, N_HEADS_B, HEAD_DIM)
    logf = jax.nn.log_sigmoid(fb.astype(jnp.float32) + b_forget.astype(jnp.float32))
    cum = jnp.cumsum(logf, axis=1)
    cum_t = jnp.swapaxes(cum, 1, 2)
    key_pos = jnp.arange(S)

    def fox_block(args):
        bi, q_blk, cq_blk = args
        q_pos = bi * Q_BLOCK + jnp.arange(Q_BLOCK)
        logit = jnp.einsum('bqhd,bshd->bhqs', q_blk, kb,
                           preferred_element_type=jnp.float32) * ATTN_SCALE
        logit = logit + jnp.swapaxes(cq_blk, 1, 2)[..., None] - cum_t[:, :, None, :]
        causal = key_pos[None, :] <= q_pos[:, None]
        logit = jnp.where(causal[None, None], logit, NEG_INF)
        p = jax.nn.softmax(logit, axis=-1).astype(vb.dtype)
        return jnp.einsum('bhqs,bshd->bqhd', p, vb)

    ob = unblock(lax.map(fox_block, (jnp.arange(nb), blocks(qb), blocks(cum))))

    ya = oa.reshape(B, S, N_HEADS_A * HEAD_DIM) @ w_out_a
    yb = ob.reshape(B, S, N_HEADS_B * HEAD_DIM) @ w_out_b
    merged = jax.nn.sigmoid(ga) * ya + jax.nn.sigmoid(gb) * yb
    return merged @ w_out

def hier_moe(h, w_group, b_group, w_router, b_router, w_e_gate, w_e_up, w_e_down):
    B, S, D = h.shape
    xt = h.reshape(B * S, D)
    N = xt.shape[0]
    g_logits = (xt @ w_group).astype(jnp.float32) + b_group.astype(jnp.float32)
    g_prob = jax.nn.softmax(g_logits, axis=-1)
    grp = jnp.argmax(g_logits, axis=-1)
    p_grp = jnp.take_along_axis(g_prob, grp[:, None], axis=1)[:, 0]
    e_logits = ((xt @ w_router).astype(jnp.float32) + b_router.astype(jnp.float32))
    e_logits = e_logits.reshape(N, N_GROUPS, EXPERTS_PER_GROUP)
    e_in = jnp.take_along_axis(e_logits, grp[:, None, None], axis=1)[:, 0]
    top_v, top_i = lax.top_k(e_in, TOPK_IN_GROUP)
    gate_w = jax.nn.softmax(top_v, axis=-1) * p_grp[:, None]
    eid = grp[:, None] * EXPERTS_PER_GROUP + top_i

    A = N * TOPK_IN_GROUP
    flat_e = eid.reshape(-1)
    flat_tok = jnp.repeat(jnp.arange(N, dtype=jnp.int32), TOPK_IN_GROUP)
    flat_w = gate_w.reshape(-1)
    order = jnp.argsort(flat_e)
    se, stok, sw = flat_e[order], flat_tok[order], flat_w[order]
    counts = jnp.bincount(flat_e, length=N_EXPERTS)
    start = jnp.cumsum(counts) - counts
    padded = (counts + EXPERT_BLOCK - 1) // EXPERT_BLOCK * EXPERT_BLOCK
    pend = jnp.cumsum(padded)
    pstart = pend - padded
    dest = pstart[se] + (jnp.arange(A) - start[se])
    P = (A + EXPERT_BLOCK - 1) // EXPERT_BLOCK * EXPERT_BLOCK + N_EXPERTS * EXPERT_BLOCK
    n_blocks = P // EXPERT_BLOCK
    tok_buf = jnp.zeros((P,), jnp.int32).at[dest].set(stok)
    w_buf = jnp.zeros((P,), jnp.float32).at[dest].set(sw)
    block_e = jnp.minimum(jnp.searchsorted(pend, jnp.arange(n_blocks) * EXPERT_BLOCK, side='right'),
                          N_EXPERTS - 1)

    def expert_block(args):
        e, toks = args
        xb = xt[toks]
        hid = jax.nn.silu(xb @ w_e_gate[e]) * (xb @ w_e_up[e])
        return hid @ w_e_down[e]

    y_buf = lax.map(expert_block, (block_e, tok_buf.reshape(n_blocks, EXPERT_BLOCK)))
    contrib = (y_buf.reshape(P, D) * w_buf[:, None]).astype(xt.dtype)
    y = jnp.zeros_like(xt).at[tok_buf].add(contrib)
    return y.reshape(B, S, D)

def setup_inputs(seed: int = 0) -> dict:
    key = jax.random.key(seed)
    ks = jax.random.split(key, 24)
    L, D = DEPTH, D_MODEL

    def nrm(k, shape, scale):
        return jax.random.normal(k, shape, jnp.float32) * scale

    x = nrm(ks[0], (BATCH, SEQ, D), 1.0)
    c = nrm(ks[1], (BATCH, D), 1.0)
    start = jax.random.randint(ks[2], (BATCH, 1), 0, 64, dtype=jnp.int32) * CHUNK
    positions = (start + jnp.arange(SEQ, dtype=jnp.int32)[None, :]).astype(jnp.int32)
    return {
        'x': x,
        'c': c,
        'positions': positions,
        'w_mod': nrm(ks[3], (L, D, 6 * D), D ** -0.5),
        'b_mod': nrm(ks[4], (L, 6 * D), 0.02),
        'g_mix': 1.0 + nrm(ks[5], (L, D), 0.02),
        'w_in': nrm(ks[6], (L, D, W_IN_COLS), D ** -0.5),
        'b_forget': 2.0 + nrm(ks[7], (L, N_HEADS_B), 0.5),
        'w_out_a': nrm(ks[8], (L, N_HEADS_A * HEAD_DIM, D), (N_HEADS_A * HEAD_DIM) ** -0.5),
        'w_out_b': nrm(ks[9], (L, N_HEADS_B * HEAD_DIM, D), (N_HEADS_B * HEAD_DIM) ** -0.5),
        'w_out': nrm(ks[10], (L, D, D), D ** -0.5),
        'g_ffn': 1.0 + nrm(ks[11], (L, D), 0.02),
        'w_group': nrm(ks[12], (L, D, N_GROUPS), D ** -0.5),
        'b_group': nrm(ks[13], (L, N_GROUPS), 0.01),
        'w_router': nrm(ks[14], (L, D, N_EXPERTS), D ** -0.5),
        'b_router': nrm(ks[15], (L, N_EXPERTS), 0.01),
        'w_e_gate': nrm(ks[16], (L, N_EXPERTS, D, D_EXPERT), D ** -0.5),
        'w_e_up': nrm(ks[17], (L, N_EXPERTS, D, D_EXPERT), D ** -0.5),
        'w_e_down': nrm(ks[18], (L, N_EXPERTS, D_EXPERT, D), D_EXPERT ** -0.5),
        'g_final': 1.0 + nrm(ks[19], (D,), 0.02),
    }

def reference(x, c, positions, w_mod, b_mod, g_mix, w_in, b_forget, w_out_a, w_out_b, w_out,
              g_ffn, w_group, b_group, w_router, b_router, w_e_gate, w_e_up, w_e_down, g_final):
    cos, sin = rope_tables(positions)
    c_act = jax.nn.silu(c)
    for l in range(DEPTH):
        mod = c_act @ w_mod[l] + b_mod[l]
        sh1, sc1, gt1, sh2, sc2, gt2 = jnp.split(mod, 6, axis=-1)
        h = modulate(rmsnorm(x, g_mix[l]), sh1, sc1)
        x = x + gt1[:, None, :] * token_mixers(h, cos, sin, w_in[l], b_forget[l],
                                               w_out_a[l], w_out_b[l], w_out[l])
        h = modulate(rmsnorm(x, g_ffn[l]), sh2, sc2)
        x = x + gt2[:, None, :] * hier_moe(h, w_group[l], b_group[l], w_router[l], b_router[l],
                                           w_e_gate[l], w_e_up[l], w_e_down[l])
    return rmsnorm(x, g_final)


_drawn_inputs = setup_inputs


def setup_inputs(seed=0):
    import zlib

    import numpy as np

    out = dict(_drawn_inputs(seed))
    spreads = {}
    factors = {'b_group': 6.754, 'b_router': 4.293, 'g_final': 2.839}
    for name, (base, spread) in spreads.items():
        noise = np.random.default_rng([zlib.crc32(name.encode()), seed]).standard_normal(out[name].shape)
        drawn = base * np.exp(spread * noise) if base else spread * noise
        out[name] = __import__('jax').numpy.asarray(drawn.astype(out[name].dtype))
    for name, factor in factors.items():
        out[name] = (out[name] * factor).astype(out[name].dtype)
    return out
```

```python
from contextlib import ExitStack

import numpy as np

import concourse.bass as bass
from concourse import mybir

F32 = mybir.dt.float32
F32R = mybir.dt.float32r
BF16 = mybir.dt.bfloat16
I32 = mybir.dt.int32
ALU = mybir.AluOpType
ACT = mybir.ActivationFunctionType
AX = mybir.AxisListType
ds = bass.ds

P = 128
D = 1024
S = 1024
KT = D // P
TT = S // P
HD = 64
NH = 8
PAIRS = NH // 2
ROPE = HD // 4
HALF = ROPE // 2
THETA = 500000.0
CHUNK = 64
TOPK = 256
NG, EPG = 4, 8
NE = NG * EPG
FE = 512
NSEL = 2
AHEAD = 4
BLOCKS = (S * NSEL + NE * P) // P
SLOTS = BLOCKS * P
EPS = 1e-6
NEG = -1e30
U = 1024

C_QA, C_KA, C_VA, C_QI, C_KI, C_WI = 0, 512, 576, 640, 1152, 1216
C_QB, C_KB, C_VB, C_F, C_GA, C_GB = 1224, 1736, 2248, 2760, 2768, 3792
P_KI, P_WI, P_KA, P_VA, P_F, P_N = 0, 64, 72, 136, 200, 208

B0 = TOPK // P
NSB = TT - B0
WB = [(b + 1) * P for b in range(TT)]
MOFF = [P * b * (b + 1) // 2 for b in range(TT)]
MTOT = P * TT * (TT + 1) // 2


FILLS = [0, 1, 2, 3, 4, 6, 8, 10]
FILLS_HEAD = 12
UNITS = 2 * TT
STEPS_IN = range(3)
STEPS_BODY = range(3, 3 + UNITS)
BIT_STEPS = 11
PJ_AT = {3: 0, 5: 1, 7: 2, 9: 3, 12: 4, 15: 5}


def unit(p, u):
    p, u = p + u // UNITS, u % UNITS
    b, z = u % TT, u // TT
    return p * UNITS + u, b, z, u, p * 2 * FILLS_HEAD, FILLS_HEAD * z + FILLS[b]


class Tally:

    def __init__(self, sem):
        self.sem, self.n, self.i, self.per, self.n0 = sem, 0, None, 0, 0

    def up(self, ins, by=1):
        ins.then_inc(self.sem, by)
        self.n += by
        return self.now()

    def now(self):
        return self.n if self.i is None else self.i * self.per + self.n

    def enter(self, i, per):
        self.i, self.per, self.n0 = i, per, self.n

    def leave(self, rounds):
        assert self.n - self.n0 == self.per, (self.n - self.n0, self.per)
        self.n = self.n0 + self.per * rounds
        self.i = None


def build(nc, x, c, positions, w_mod, b_mod, g_mix, w_in, b_forget, w_out_a, w_out_b, w_out, g_ffn,
          w_group, b_group, w_router, b_router, w_e_gate, w_e_up, w_e_down, g_final, out):
    w_in_v = w_in[0].rearrange("(t p) n -> p t n", p=P)
    w_mod_v = w_mod[0].rearrange("(t p) n -> p t n", p=P)
    x_v = x[0].rearrange("(t p) d -> t p d", p=P)

    h2_d = nc.dram_tensor("h2_rows", (S, D), F32).ap()
    slot_d = nc.dram_tensor("slot_rows", ((BLOCKS + 2) * P, 4), I32).ap()
    y_d = nc.dram_tensor("sum_rows", (S + P, D), F32).ap()
    cum_d = nc.dram_tensor("cum_rows", (2, NH, S), F32).ap()

    with ExitStack() as ctx:
        def sb(name, shape, dt=F32):
            return ctx.enter_context(nc.sbuf_tensor(name, shape, dt))

        def sem(name):
            return ctx.enter_context(nc.semaphore(name))

        ident = sb("ident", [P, P])
        upper = sb("upper", [P, P])
        ones = sb("ones", [P, P])
        small = sb("small", [P, 600])
        with nc.sbuf_tensor("arena", [P, 51 * U], F32) as arena:
            pass
        rounded = [sb(f"rounded{u}", [P, U], F32R) for u in range(51)]

        def at(u, n, shape=None):
            a = arena[:, int(u * U):int(u * U) + n]
            if shape is not None:
                names = " ".join(f"a{k}" for k in range(len(shape)))
                a = a.rearrange(f"p ({names}) -> p {names}", **{f"a{k}": s for k, s in enumerate(shape)})
            return a

        ps = ctx.enter_context(nc.psum_tensor("ps", [P, 8, 512], F32))

        used = [0]

        def sm(n, shape=None):
            a = small[:, used[0]:used[0] + n]
            used[0] += n
            if shape is not None:
                names = " ".join(f"a{k}" for k in range(len(shape)))
                a = a.rearrange(f"p ({names}) -> p {names}", **{f"a{k}": s for k, s in enumerate(shape)})
            return a

        cT = sm(KT)
        sil = sm(KT)
        bmod = sm(16)
        gmix = sm(KT)
        a1 = sm(KT)
        sh1 = sm(KT)
        ssq = sm(TT)
        rstd = sm(TT)
        wi = sm(TT * NH, [TT, NH])
        thr_bits, cand, cnt, kneed, sigma, bitt = sm(NSB), sm(NSB), sm(NSB), sm(NSB), sm(NSB), sm(1)
        wm = sm(NSB)
        rs = sm(16)
        rinv = sm(16)

        hT = at(0, 8 * U, [KT, S])
        xs = at(37, 8 * U, [TT, D])
        wslot = [at(8, 4 * U, [KT, 512]), at(12, 4 * U, [KT, 512])]
        wsmall = at(8, KT * P_N, [KT, P_N])
        wqi = wslot[1]
        acc = [at(49, U), at(50, U)] + [at(45 + j, U) for j in range(4)]
        mod2 = [at(37, 4 * U, [KT, 512]), at(41, 4 * U, [KT, 512])]
        qiT = at(21, 4 * U, [4, S])
        kT = at(25, 4 * U, [4, S])
        va = at(29, U, [TT, 2, HD])
        relu = [at(30, U), at(31, U)]
        qtm = [at(32, 512, [NH, HD]), at(32.5, 512, [NH, HD])]
        ktm = [at(33, 512, [4, P]), at(33.5, 512, [4, P])]
        kraw = [at(35, P_N), at(35.21875, P_N)]
        rt = [at(34, 128 * 2, [2, NH, ROPE]), at(34.25, 128 * 2, [2, NH, ROPE])]
        rk = [at(34.5, 64, [2, 2, ROPE]), at(34.5 + 1 / 16, 64, [2, 2, ROPE])]
        fall = at(34.75, 64, [TT, NH])
        fe = at(34.75 + 1 / 16, 64, [TT, NH])
        fl = at(34.75 + 2 / 16, 64, [TT, NH])
        fx = at(34.75 + 3 / 16, 64, [TT, NH])
        cum = sm(64, [TT, NH])
        bfb = sm(8)
        pos = sm(TT)
        ang = at(35.5 + 4 / 16, TT * HALF, [TT, HALF])
        angk = at(35.5 + 5 / 16, TT * HALF, [TT, HALF])
        angr = at(35.5 + 6 / 16, TT * HALF, [TT, HALF])
        cos2 = sm(TT * ROPE, [TT, 2, HALF])
        sin2 = sm(TT * ROPE, [TT, 2, HALF])
        invf = sm(HALF)
        posi = sm(TT).bitcast(I32)
        cumT = at(36, 2 * U, [2, S])
        sc = at(16, MTOT)

        aq = [at(21 + z, U) for z in range(2)]
        ak = [at(23 + z, U) for z in range(2)]
        raw = [at(25, U), at(26, U)]
        vall = at(11, 4 * U, [PAIRS, TT, P])
        wB = [at(8 + j, U, [KT, P]) for j in range(3)]
        lg = [at(u, U) for u in (30, 32, 33, 34)]
        pT = [at(35 + j, U) for j in range(2)]
        window = at(15, U)
        ob = at(37, 4 * U, [TT, NH * HD])
        oa = at(21, 4 * U, [TT, NH * HD])
        junk = [at(49 + j / 2, 512).bitcast(BF16) for j in range(2)]
        eqt, pre, selt = at(12, U), at(13, U), at(50, U)
        nmax = sm(16)
        wqa = at(8, 4 * U, [KT, 512])
        atm = [at(31 + z / 2, 512, [NH, HD]) for z in range(2)]
        art = [at(49 + z / 4, 256, [2, NH, ROPE]) for z in range(2)]
        qaT = at(41, 4 * U, [4, S])
        qcur = [at(25 + z, U) for z in range(2)]

        bmb = at(8, 4 * U, [4, D])
        gffn = at(14, U)
        gt1, sh2, a2, gt2 = acc[2:6]
        oT = at(16, 8 * U, [2 * 4, S])
        wO = [[at(8 + 3 * z, U, [KT, P]), at(9 + 3 * z, U, [KT, P]), at(10 + 3 * z, 512, [4, P]), at(10.5 + 3 * z, 512, [4, P])]
              for z in range(2)]
        eg = [at(32 + z, U) for z in range(2)]
        mT = at(24, 8 * U, [KT, S])
        wout = at(34, 8 * U, [KT, D])
        h_hi = [rounded[u][:] for u in (15, 41, 42, 43, 44, 49, 50, 14)]
        h_lo = [rounded[kt][:] for kt in range(KT)]
        w_hi = [[rounded[34 + 2 * z + g][:] for g in range(2)] for z in range(2)]
        w_lo = [[rounded[8 + 3 * z + g][:] for g in range(2)] for z in range(2)]
        x1 = at(0, 8 * U, [TT, D])
        ytmp = [at(42 + z, U) for z in range(2)]
        sqj = at(44, U)
        h2 = [at(8 + z, U) for z in range(2)]
        h2T = [at(10 + z, U, [KT, P]) for z in range(2)]
        wgr = at(12, KT * (NG + NE), [KT, NG + NE])
        bgr = at(12.5, NG + NE)
        lgt = at(12.75 - 1 / 8, TT * (NG + NE), [TT, NG + NE])
        doff = [13 * U]

        def dsp(n, shape=None):
            a = at(doff[0] / U, n, shape)
            doff[0] += n
            return a

        gmx, kmin, pgr, v1, v2, ee = (dsp(TT) for _ in range(6))
        g12 = dsp(2 * TT, [2, TT])
        key4, oh4, ex4 = (dsp(TT * NG, [TT, NG]) for _ in range(3))
        ein, key8 = (dsp(TT * EPG, [TT, EPG]) for _ in range(2))
        oh8 = [dsp(TT * EPG, [TT, EPG]) for _ in range(2)]
        em = dsp(TT * NE, [TT, NE])
        ohe = [dsp(TT * NE, [TT, NE]) for _ in range(2)]
        mb = dsp(TT * NE // 2).bitcast(BF16).rearrange("q (t e) -> q t e", t=TT)
        mx = dsp((TT + 1) * NE // 2).bitcast(BF16).rearrange("q (t e) -> q t e", t=TT + 1)
        strict = dsp(P // 2).bitcast(BF16)
        oneb = dsp(P // 2).bitcast(BF16)
        nbi, nbf, pst = (dsp(NE) for _ in range(3))
        i4, i8 = dsp(NG), dsp(EPG)
        assert doff[0] <= 16 * U
        cmpb = at(43, BLOCKS * NE, [BLOCKS, NE])
        ib = at(44.5, BLOCKS)
        bef = at(44.5 + 1 / 16, BLOCKS)
        pend = at(44.5 + 2 / 16 + 1 / 64, NE)
        dstf = at(44.5 + 2 / 16, 2 * TT, [2, TT])
        dsti = at(44.5 + 3 / 16, 2 * TT, [2, TT]).bitcast(I32)
        slt = at(44.5 + 4 / 16, 2 * TT * 4, [2, TT, 4]).bitcast(I32)
        dflt = at(41.5, (BLOCKS + 2) * 4, [BLOCKS + 2, 4]).bitcast(I32)
        cmpr, blkr = at(49, NE * NE, [NE, NE]), at(50, NE * NE, [NE, NE])
        nonempty, runs_to, begins = (at(44.5 + (5 + k) / 16, NE) for k in range(3))
        run_of = upper[:, 0:BLOCKS].bitcast(I32)
        n_used = upper[:, BLOCKS:BLOCKS + 1].bitcast(I32)
        run_e = upper[:, BLOCKS + 1:BLOCKS + 1 + NE].bitcast(I32)
        run_free = upper[:, BLOCKS + 1 + NE:BLOCKS + 1 + 2 * NE].bitcast(I32)
        n_runs = upper[:, BLOCKS + 1 + 2 * NE:BLOCKS + 2 + 2 * NE].bitcast(I32)
        SET = 12 * U
        wE = [[at(8 + 12 * z + 4 * j, 4 * U, [KT, FE] if j < 2 else [FE // P, D]) for j in range(3)] for z in range(2)]
        xg = [at(32 + z, U) for z in range(2)]
        xT = [at(34 + z, U, [KT, P]) for z in range(2)]
        sg = [at(36 + z / 2, 512) for z in range(2)]
        hid = [at(37 + z / 2, 512) for z in range(2)]
        hidT = [at(38 + z / 2, 512, [4, P]) for z in range(2)]
        ye = [at(39 + z, U) for z in range(2)]
        idx = [at(41 + q / 64, 4).bitcast(I32) for q in range(AHEAD)]
        gfin = acc[2]

        bmb_in = sem("bmb_in")
        mbc_ps = sem("mbc_ps")
        mbc_ok = sem("mbc_ok")
        ot_ps = sem("ot_ps")
        ot_act = sem("ot_act")
        ot_dve = sem("ot_dve")
        wo_in = [sem(f"wo_in{z}") for z in range(2)]
        g_ps = sem("g_ps")
        yab_ps = sem("yab_ps")
        g_exp = sem("g_exp")
        mg_done = sem("mg_done")
        wout_in = [sem(f"wout_in{c}") for c in range(4)]
        hhi_ok = sem("hhi_ok")
        hlo_ok = sem("hlo_ok")
        whi_ok = sem("whi_ok")
        wlo_ok = sem("wlo_ok")
        y_ps = sem("y_ps")
        x1_ok = sem("x1_ok")
        yt_ok = sem("yt_ok")
        sq2_ok = sem("sq2_ok")
        ms2_ok = sem("ms2_ok")
        sqrt2_ok = sem("sqrt2_ok")
        h2_ok = sem("h2_ok")
        h2_out = [sem(f"h2_out{z}") for z in range(2)]
        h2t_ps = sem("h2t_ps")
        h2t_ok = sem("h2t_ok")
        r_in = sem("r_in")
        lg_ps = sem("lg_ps")
        lg_ok = sem("lg_ok")
        dc_ok = sem("dc_ok")
        x1_out = sem("x1_out")
        g_sub = sem("g_sub")
        g_e = sem("g_e")
        d_sub = sem("d_sub")
        d_e = sem("d_e")
        m_ok = sem("m_ok")
        rank_ps = sem("rank_ps")
        dest_ok = sem("dest_ok")
        dflt_out = sem("dflt_out")
        slot_out = sem("slot_out")
        used_ok = sem("used_ok")
        wE_in = [[sem(f"wE_in{z}{j}") for j in range(3)] for z in range(2)]
        gf_in = sem("gf_in")
        idx_in = [sem(f"idx_in{z}") for z in range(2)]
        xg_in = [sem(f"xg_in{z}") for z in range(2)]
        xt_e = sem("xt_e")
        xt_c = sem("xt_c")
        gate_ps = sem("gate_ps")
        up_ps = sem("up_ps")
        gexp_e = sem("gexp_e")
        hid_ok = sem("hid_ok")
        ht_ps = sem("ht_ps")
        ht_ok = sem("ht_ok")
        down_ps = sem("down_ps")
        ye_ok = sem("ye_ok")
        y_out = [sem(f"y_out{z}") for z in range(2)]
        y_all = sem("y_all")
        f_sq = sem("f_sq")
        f_ms = sem("f_ms")
        f_rt = sem("f_rt")
        f_ok = sem("f_ok")
        out_ok = sem("out_ok")
        win_ok = sem("win_ok")
        aug1_ok = sem("aug1_ok")
        row_in = [sem(f"row_in{z}") for z in range(2)]
        wb_in = [sem(f"wb_in{j}") for j in range(3)]
        pj_ps = sem("pj_ps")
        pj_out = sem("pj_out")
        aug_ok = sem("aug_ok")
        qk_done = sem("qk_done")
        lg_done = sem("lg_done")
        p_done = sem("p_done")
        t_done = sem("t_done")
        pt_copied = sem("pt_copied")
        pv_done = sem("pv_done")
        o_done = sem("o_done")
        wqa_in = sem("wqa_in")
        qa_ps = sem("qa_ps")
        qa_tm = sem("qa_tm")
        qa_rope = sem("qa_rope")
        qa_tp = sem("qa_tp")
        qa_out = sem("qa_out")
        qc_ok = sem("qc_ok")
        c_in = sem("c_in")
        x_in = [sem(f"x_in{t}") for t in range(TT)]
        mod_in = [sem(f"mod_in{k}") for k in range(4)]
        wi_in = [sem(f"wi_in{k}") for k in range(2)]
        stand = sem("stand")
        consts = sem("consts")
        freq_ok = sem("freq_ok")
        pool_chain = sem("pool_chain")
        dve_chain = sem("dve_chain")
        act_chain = sem("act_chain")
        silu_e = sem("silu_e")
        silu_ok = sem("silu_ok")
        ssq_ok = sem("ssq_ok")
        ms_ok = sem("ms_ok")
        sqrt_ok = sem("sqrt_ok")
        xn_ok = sem("xn_ok")
        acc_ok = sem("acc_ok")
        modp_ok = sem("modp_ok")
        mod1_ok = sem("mod1_ok")
        xt_ps = sem("xt_ps")
        xt_act = sem("xt_act")
        xt_dve = sem("xt_dve")
        ang_ok = sem("ang_ok")
        sin_ok = sem("sin_ok")
        ip_ps = sem("ip_ps")
        q_copied = sem("q_copied")
        k_spread = sem("k_spread")
        rope_ok = sem("rope_ok")
        it_ps = sem("it_ps")
        it_copied = sem("it_copied")
        f_ready = sem("f_ready")
        f_exp = sem("f_exp")
        f_ln = sem("f_ln")
        f_pre = sem("f_pre")
        cum_ps = sem("cum_ps")
        cum_sb = sem("cum_sb")
        cumt_ps = sem("cumt_ps")
        cumt_sb = sem("cumt_sb")
        cum_out = sem("cum_out")
        rel_ps = sem("rel_ps")
        relu_ok = sem("relu_ok")
        score_ok = sem("score_ok")
        zero_ok = sem("zero_ok")

        N_IU = NSB * NH

        block = ctx.enter_context(nc.Block())

        @block.sync
        def _(sp):
            sp.dma_start(cT, c.rearrange("o (t p) -> p (o t)", p=P), allow_slow_non_contiguous=True).then_inc(c_in, 16)
            sp.dma_start(bmod, b_mod[0, 0:2 * D].rearrange("(t p) -> p t", p=P), allow_slow_non_contiguous=True).then_inc(c_in, 16)
            sp.dma_start(gmix, g_mix[0].rearrange("(t p) -> p t", p=P), allow_slow_non_contiguous=True).then_inc(c_in, 16)
            sp.dma_start(posi, positions[0].rearrange("(t p) -> p t", p=P), allow_slow_non_contiguous=True).then_inc(c_in, 16)
            sp.dma_start(bfb, b_forget[0:1, :].to_broadcast([P, NH])).then_inc(c_in, 16)
            for n in range(2):
                sp.dma_start(wslot[n], w_mod_v[:, :, n * 512:(n + 1) * 512]).then_inc(mod_in[n], 16)
            for t in range(TT):
                sp.dma_start(xs[:, t, :], x_v[t]).then_inc(x_in[t], 16)
            for n in range(2, 4):
                sp.wait_ge(acc_ok, n - 1)
                sp.dma_start(wslot[n % 2], w_mod_v[:, :, n * 512:(n + 1) * 512]).then_inc(mod_in[n % 2], 16)
            sp.wait_ge(acc_ok, 3)
            for a, b, n in ((C_KI, P_KI, 72), (C_KA, P_KA, 128), (C_F, P_F, NH)):
                sp.dma_start(wsmall[:, :, b:b + n], w_in_v[:, :, a:a + n], allow_slow_non_contiguous=True).then_inc(wi_in[0], 16)
            sp.wait_ge(acc_ok, 4)
            sp.dma_start(wqi, w_in_v[:, :, C_QI:C_QI + 512]).then_inc(wi_in[1], 16)
            sp.wait_ge(xt_ps, 16)
            for n in range(4, 12):
                if n >= 6:
                    sp.wait_ge(acc_ok, n - 1)
                sp.dma_start(mod2[n % 2], w_mod_v[:, :, n * 512:(n + 1) * 512]).then_inc(mod_in[2 + n % 2], 16)
            sp.wait_ge(ip_ps, TT)
            for j in range(3):
                sp.dma_start(wB[j], w_in_v[:, :, (C_QB, C_KB, C_VB)[j]:(C_QB, C_KB, C_VB)[j] + P]).then_inc(wb_in[j], 16)
            sp.wait_ge(cumt_sb, 2)
            sp.dma_start(cum_d[0], cumT[0:NH, 0, :]).then_inc(cum_out, 16)
            sp.dma_start(cum_d[1], cumT[0:NH, 1, :]).then_inc(cum_out, 16)
            sp.wait_ge(cum_out, 32)

            def rows(p, z, head):
                sp.dma_start(aq[z][HD + 1:HD + 2, :], cum_d[0, ds(head, 1), :]).then_inc(row_in[z], 16)
                sp.dma_start(ak[z][HD:HD + 1, :], cum_d[1, ds(head, 1), :]).then_inc(row_in[z], 16)

            def weights_b(p, j):
                col = (C_QB, C_KB, C_VB)[j]
                sp.dma_start(wB[j], w_in_v[:, :, ds(p * P + col, P)]).then_inc(wb_in[j], 16)

            sp.wait_ge(aug1_ok, 4)
            for z in range(2):
                rows(0, z, z)
            for j in range(3):
                sp.wait_ge(pj_ps, 2 * j + 2)
                weights_b(1, j)

            def next_pair(p, more):
                if more:
                    sp.wait_ge(pj_ps, 6 * p + 2)
                    weights_b(p + 1, 0)
                sp.wait_ge(qk_done, UNITS * (p - 1) + TT)
                rows(p, 0, 2 * p)
                if more:
                    for j in (1, 2):
                        sp.wait_ge(pj_ps, 6 * p + 2 * j + 2)
                        weights_b(p + 1, j)
                sp.wait_ge(qk_done, UNITS * p)
                rows(p, 1, 2 * p + 1)

            with sp.Fori(1, PAIRS - 1) as p:
                next_pair(p, True)
            next_pair(PAIRS - 1, False)
            sp.wait_ge(pj_ps, 6 * PAIRS)
            sp.dma_start(wqa, w_in_v[:, :, C_QA:C_QA + 512]).then_inc(wqa_in, 16)
            sp.wait_ge(qa_ps, TT)
            for q in range(4):
                sp.dma_start(bmb[:, q, :], b_mod[0:1, (2 + q) * D:(3 + q) * D].to_broadcast([P, D])).then_inc(bmb_in, 16)
            sp.wait_ge(pv_done, UNITS * PAIRS + 3)
            sp.dma_start(gffn, g_ffn[0:1, :].to_broadcast([P, D])).then_inc(bmb_in, 16)

            def weights_o(m, z):
                sp.dma_start(wO[z][0], w_in_v[:, :, ds(m * P + C_GA, P)]).then_inc(wo_in[z], 16)
                sp.dma_start(wO[z][1], w_in_v[:, :, ds(m * P + C_GB, P)]).then_inc(wo_in[z], 16)
                sp.dma_start(wO[z][2], w_out_a[0].rearrange("(t q) n -> q t n", q=P)[:, :, ds(m * P, P)]).then_inc(wo_in[z], 16)
                sp.dma_start(wO[z][3], w_out_b[0].rearrange("(t q) n -> q t n", q=P)[:, :, ds(m * P, P)]).then_inc(wo_in[z], 16)

            sp.wait_ge(mbc_ok, 9)
            for z in range(2):
                weights_o(z, z)
            with sp.Fori(0, KT // 2 - 1) as i:
                for z in range(2):
                    sp.wait_ge(yab_ps, 4 * i + 2 * z + 2)
                    weights_o(2 * i + 2 + z, z)
            sp.wait_ge(g_ps, 2 * KT)
            for k in range(4):
                sp.dma_start(wout[:, 2 * k:2 * k + 2, :], w_out[0].rearrange("(t q) n -> q t n", q=P)[:, 2 * k:2 * k + 2, :]).then_inc(wout_in[k], 16)
            for t in range(TT):
                sp.dma_start(x1[:, t, :], x_v[t]).then_inc(x_in[t], 16)
            sp.wait_ge(yab_ps, 2 * KT)
            sp.dma_start(wgr[:, :, 0:NG], w_group[0].rearrange("(t q) n -> q t n", q=P), allow_slow_non_contiguous=True).then_inc(r_in, 16)
            sp.dma_start(wgr[:, :, NG:NG + NE], w_router[0].rearrange("(t q) n -> q t n", q=P), allow_slow_non_contiguous=True).then_inc(r_in, 16)
            sp.dma_start(bgr[:, 0:NG], b_group[0:1, :].to_broadcast([P, NG])).then_inc(r_in, 16)
            sp.dma_start(bgr[:, NG:NG + NE], b_router[0:1, :].to_broadcast([P, NE])).then_inc(r_in, 16)
            for t in range(TT):
                sp.wait_ge(x1_ok, 2 * t + 2)
                sp.dma_start(y_d[t * P:(t + 1) * P, :], x1[:, t, :]).then_inc(x1_out, 16)
                if t == 0:
                    sp.dma_start(y_d[S:S + P, :], x1[:, t, :]).then_inc(x1_out, 16)
                sp.wait_ge(h2_ok, t + 1)
                sp.dma_start(h2_d[t * P:(t + 1) * P, :], h2[t % 2]).then_inc(h2_out[t % 2], 16)
            sp.wait_ge(x1_ok, 2 * TT)
            sp.dma_start(gfin, g_final.rearrange("(o n) -> o n", o=1).to_broadcast([P, D])).then_inc(gf_in, 16)
            sp.wait_ge(used_ok, 1)
            for z in range(2):
                sp.wait_ge(h2_out[z], 16 * TT // 2)
            runs = sp.value_load(n_runs[0:1, :], min_val=1, max_val=NE)
            with sp.Fori(0, NE // 2) as i:
                for z in range(2):
                    r = 2 * i + z
                    with sp.If(r < runs):
                        e = sp.value_load(run_e[0:1, ds(r, 1)], min_val=0, max_val=NE - 1)
                        free = sp.value_load(run_free[0:1, ds(r, 1)], min_val=1, max_val=BLOCKS + 2)
                        for j, (w, read) in enumerate(((w_e_gate, gate_ps), (w_e_up, up_ps), (w_e_down, down_ps))):
                            sp.wait_ge(read, free)
                            sp.dma_start(wE[z][j], w[0, ds(e, 1)].rearrange("o (q t) n -> q (o t) n", q=P)).then_inc(wE_in[z][j], 16)
                    sp.nop()
            sp.wait_ge(y_all, 1)
            for t in range(TT):
                sp.dma_start(x1[:, t, :], y_d[t * P:(t + 1) * P, :]).then_inc(x_in[t], 16)
            for t in range(TT):
                sp.wait_ge(f_ok, t + 1)
                sp.dma_start(out[0].rearrange("(t q) d -> t q d", q=P)[t], x1[:, t, :]).then_inc(out_ok, 16)
            sp.wait_ge(out_ok, 16 * TT)

        @block.gpsimd
        def _(pool):
            chain = Tally(pool_chain)

            def link(ins):
                pool.wait_ge(pool_chain, chain.up(ins))

            for j in range(HALF):
                pool.memset(invf[:, j:j + 1], float(np.float32(THETA) ** np.float32(-2 * j / ROPE))).then_inc(freq_ok, 1)
            for b in range(NSB):
                pool.memset(wm[:, b:b + 1], float(WB[B0 + b] - TOPK + 1)).then_inc(zero_ok, 1)

            pool.memset(ident[:], 0.0).then_inc(pool_chain, 1)
            pool.memset(upper[:], 1.0).then_inc(pool_chain, 1)
            pool.memset(ones[:], 1.0).then_inc(consts, 1)
            chain.n = 2
            pool.wait_ge(pool_chain, 2)
            pool.affine_select(out=ident[:], in_=ident[:], compare_op=ALU.not_equal, fill=1.0, base=0,
                               pattern=[[-1, P]], channel_multiplier=1).then_inc(consts, 1)
            pool.affine_select(out=upper[:], in_=upper[:], compare_op=ALU.is_ge, fill=0.0, base=0,
                               pattern=[[1, P]], channel_multiplier=-1).then_inc(consts, 1)
            for j in range(2):
                pool.memset(ktm[j].rearrange("p a b -> p (a b)"), 0.0).then_inc(consts, 1)
            pool.wait_ge(c_in, 80)
            pool.wait_ge(consts, 5)
            for t in range(TT):
                pool.wait_ge(q_copied, 2 * t + 1)
                if t >= 2:
                    pool.wait_ge(it_ps, t - 1)
                for j, col in enumerate((P_KI, P_KA)):
                    for z in range(2):
                        chain.up(pool.tensor_copy(ktm[t % 2][:, 2 * j + z, z * HD + ROPE:(z + 1) * HD],
                                                  kraw[t % 2][:, col + ROPE:col + HD]))
                for z in range(2):
                    chain.up(pool.tensor_copy(va[:, t, z, :], kraw[t % 2][:, P_VA:P_VA + HD]))
                chain.up(pool.tensor_scalar(wi[:, t, :], kraw[t % 2][:, P_WI:P_WI + NH], float(np.float32(NH ** -0.5)), None, ALU.mult))
                pool.wait_ge(pool_chain, chain.now())
                pool.tensor_tensor(fall[:, t, :], kraw[t % 2][:, P_F:P_F + NH], bfb, ALU.add).then_inc(k_spread, 1)
            pool.wait_ge(ip_ps, TT)
            link(pool.memset(window, 0.0))
            pool.affine_select(out=window[:, S - P:S], in_=window[:, S - P:S], compare_op=ALU.is_ge, fill=NEG, base=0,
                               pattern=[[-1, P]], channel_multiplier=1).then_inc(win_ok, 1)
            link(pool.memset(sc[:, 0:MOFF[B0]], 0.0))
            for b in range(B0):
                pool.memset(sc[0:CHUNK, MOFF[b] + WB[b] - CHUNK:MOFF[b] + WB[b]], NEG).then_inc(win_ok, 1)
            pool.wait_ge(rel_ps, N_IU)
            for z in range(2):
                pool.memset(aq[z][HD:HD + 2, :], 1.0).then_inc(aug1_ok, 1)
                pool.memset(ak[z][HD:HD + 2, :], 1.0).then_inc(aug1_ok, 1)

            with pool.Fori(1, PAIRS) as p:
                for z in range(2):
                    pool.wait_ge(qk_done, UNITS * (p - 1) + TT * (z + 1))
                    for j, dst in enumerate((aq, ak)):
                        pool.wait_ge(pj_out, 6 * p + 2 * j + 2)
                        pool.wait_ge(aug_ok, 4 * p + 2 * z + j)
                        pool.sem_inc(stand, 1)
                        pool.tensor_copy(dst[z][0:HD, :], raw[j][z * HD:(z + 1) * HD, :]).then_inc(aug_ok, 1)
            pool.wait_ge(qa_out, TT)
            with pool.Fori(1, PAIRS) as p:
                for z in range(2):
                    pool.wait_ge(qk_done, UNITS * (PAIRS - 1 + p) + TT * (z + 1))
                    pool.sem_inc(stand, 1)
                    pool.tensor_copy(qcur[z], qaT[:, ds(p, 1), :].rearrange("q a s -> q (a s)")).then_inc(qc_ok, 1)
            pool.wait_ge(yab_ps, 2 * KT)
            pool.wait_ge(x1_ok, 2 * TT)
            pool.wait_ge(sq2_ok, TT)
            chain.up(pool.memset(strict, 1.0))
            chain.up(pool.memset(oneb, 1.0))
            chain.up(pool.iota(i4, [[1, NG]], base=0, channel_multiplier=0, allow_small_or_imprecise_dtypes=True))
            chain.up(pool.iota(i8, [[1, EPG]], base=0, channel_multiplier=0, allow_small_or_imprecise_dtypes=True))
            chain.up(pool.iota(ib, [[1, BLOCKS]], base=0, channel_multiplier=0, allow_small_or_imprecise_dtypes=True))
            chain.up(pool.iota(slt[:, :, :, 0], [[0, 2], [P, TT]], base=0, channel_multiplier=1))
            chain.up(pool.iota(slt[:, :, :, 1], [[0, 2], [P, TT]], base=0, channel_multiplier=1))
            chain.up(pool.memset(slt[:, :, :, 3], 0))
            link(pool.memset(dflt, 0))
            link(pool.iota(dflt[:, :, 1], [[0, BLOCKS + 2]], base=S, channel_multiplier=1))
            pool.affine_select(out=strict, in_=strict, compare_op=ALU.is_gt, fill=0.0, base=0,
                               pattern=[[1, P]], channel_multiplier=-1).then_inc(dc_ok, 1)
            pool.dma_start(slot_d.rearrange("(b q) f -> q b f", q=P), dflt, allow_slow_non_contiguous=True).then_inc(dflt_out, 16)
            pool.wait_ge(dflt_out, 16)
            pool.wait_ge(dest_ok, 1)
            for k in range(2):
                for t in range(TT):
                    pool.indirect_dma_start(slot_d, bass.IndirectOffsetOnAxis(dsti[:, k, t:t + 1], 0), slt[:, k, t, :], None).then_inc(slot_out, 16)
            pool.wait_ge(slot_out, 16 * 2 * TT)
            for z in range(2):
                pool.wait_ge(h2_out[z], 16 * TT // 2)

            def rows_of(b, q):
                pool.dma_start(idx[q % AHEAD], slot_d[ds(b * P, P), :], allow_slow_non_contiguous=True).then_inc(idx_in[q % 2], 16)

            pool.wait_ge(used_ok, 2)
            used = pool.value_load(n_used[0:1, :], min_val=1, max_val=BLOCKS)
            for q in range(2):
                rows_of(q, q)
            pool.wait_ge(idx_in[0], 16)
            pool.indirect_dma_start(xg[0], None, h2_d, bass.IndirectOffsetOnAxis(idx[0][:, 0:1], 0)).then_inc(xg_in[0], 16)
            pool.wait_ge(x1_out, 16 * (TT + 1))
            with pool.Fori(0, BLOCKS // AHEAD) as i:
                for q in range(AHEAD):
                    b, z = AHEAD * i + q, q % 2
                    with pool.If(b < used):
                        pool.wait_ge(idx_in[1 - z], 32 * i + 16 * ((q + 1) // 2 + 1))
                        pool.wait_ge(xt_e, b)
                        pool.sem_inc(stand, 1)
                        pool.indirect_dma_start(xg[1 - z], None, h2_d, bass.IndirectOffsetOnAxis(idx[(q + 1) % AHEAD][:, 0:1], 0)).then_inc(xg_in[1 - z], 16)
                        pool.wait_ge(y_out[z], 32 * i + 16 * (q // 2))
                        rows_of(b + 2, q + 2)
                        pool.wait_ge(y_out[1 - z], 32 * i + 16 * ((q + 1) // 2))
                        pool.wait_ge(ye_ok, b + 1)
                        pool.sem_inc(stand, 1)
                        pool.indirect_dma_start(y_d, bass.IndirectOffsetOnAxis(idx[q][:, 1:2], 0), ye[z], None, compute_op=ALU.add).then_inc(y_out[z], 16)
                    pool.nop()
            for z in range(2):
                pool.wait_ge(y_out[z], (used + (1 - z)) // 2 * 16)
            pool.sem_inc(y_all, 1)

        @block.scalar
        def _(act):
            chain = Tally(act_chain)

            def link(ins):
                act.wait_ge(act_chain, chain.up(ins))

            act.wait_ge(c_in, 80)
            act.activation(sil, cT, ACT.Exp, scale=-1.0).then_inc(silu_e, 1)
            for t in range(TT):
                act.wait_ge(x_in[t], 16)
                if t >= 2:
                    act.wait_ge(ssq_ok, t - 1)
                act.activation(relu[t % 2], xs[:, t, :], ACT.Square, accum_out=ssq[:, t:t + 1]).then_inc(ssq_ok, 1)
            act.wait_ge(ms_ok, 1)
            act.activation(rstd, ssq, ACT.Sqrt).then_inc(sqrt_ok, 1)
            act.wait_ge(ang_ok, 1)
            act.activation(sin2[:, :, 0, :], angr, ACT.Sin).then_inc(sin_ok, 1)
            act.activation(cos2[:, :, 0, :], angr, ACT.Sin, scale=0.5).then_inc(sin_ok, 1)
            act.wait_ge(mod1_ok, 2)
            for n in range(0, 16, 2):
                act.wait_ge(xt_ps, n + 1)
                kt, half = n // 2, n % 2
                act.activation(hT[:, kt, half * 512:(half + 1) * 512], ps[:, n % 7, :], ACT.Identity,
                               bias=sh1[:, kt:kt + 1], scale=a1[:, kt:kt + 1]).then_inc(xt_act, 1)
            act.wait_ge(consts, 5)

            def project_out(t):
                act.wait_ge(ip_ps, t + 1)
                if t >= 2:
                    act.wait_ge(it_ps, t - 1)
                    act.wait_ge(rope_ok, t - 1)
                    act.wait_ge(k_spread, t - 1)
                act.activation(kraw[t % 2], ps[:, t % 2, 0:P_N], ACT.Copy).then_inc(q_copied, 1)
                act.activation(qtm[t % 2].rearrange("p h d -> p (h d)"), ps[:, 2 + t % 2, :], ACT.Copy).then_inc(q_copied, 1)

            def turned_out(t):
                act.wait_ge(it_ps, t + 1)
                act.activation(qiT[:, :, t * P:(t + 1) * P], ps[:, 4 + t % 2, :].rearrange("p (j m) -> p j m", j=4),
                               ACT.Copy).then_inc(it_copied, 1)
                act.activation(kT[:, :, t * P:(t + 1) * P], ps[:, 6 + t % 2, :].rearrange("p (j m) -> p j m", j=4),
                               ACT.Copy).then_inc(it_copied, 1)

            for t in range(TT + 1):
                if t < TT:
                    project_out(t)
                if t >= 1:
                    turned_out(t - 1)
            act.wait_ge(f_ready, 1)
            act.activation(fl, fe, ACT.Exp, scale=-1.0).then_inc(f_exp, 1)
            act.wait_ge(f_exp, 1)
            act.activation(fe, fl, ACT.Ln, bias=1.0).then_inc(f_ln, 1)
            for n in range(N_IU):
                w = WB[B0 + n // NH]
                act.wait_ge(rel_ps, n + 1)
                if n >= 2:
                    act.wait_ge(score_ok, n - 1)
                b = 2 * (n % 4)
                act.activation(relu[n % 2][:, 0:w], ps[:, b:b + 2, :].rearrange("p a b -> p (a b)")[:, 0:w], ACT.Relu,
                               scale=float(HD ** -0.5)).then_inc(relu_ok, 1)


            def pj_evac(p, g, first):
                act.wait_ge(pj_ps, 6 * p + g + 1)
                j, half = g // 2, g % 2
                if first:
                    act.wait_ge(rel_ps, N_IU)
                    act.wait_ge(it_copied, 2 * TT)
                elif j < 2:
                    act.wait_ge(aug_ok, 4 * (p - 1) + 3 + j)
                if j < 2:
                    dst = raw[j][:, half * 512:(half + 1) * 512]
                else:
                    dst = vall[:, ds(p, 1), 4 * half:4 * half + 4, :].rearrange("q o a n -> q (o a n)")
                act.activation(dst, ps[:, 7, :], ACT.Copy, scale=float(HD ** -0.5) if j == 1 else 1.0).then_inc(pj_out, 1)

            def attend(p, steps, more, filler):
                for s in steps:
                    if s < UNITS or more:
                        n, b, z, u, _, _ = unit(p, s)
                        act.wait_ge(lg_done, n + 3)
                        buf = lg[u % 4]
                        act.activation(buf[:, 0:WB[b]], buf[:, 0:WB[b]], ACT.Exp, bias=nmax[:, u:u + 1], scale=-1.0,
                                       accum_out=rs[:, u:u + 1]).then_inc(p_done, 1)
                    if s in filler:
                        filler[s]()
                    if s >= 2 and (s - 2 < UNITS or more):
                        n, b, z, u, f0, fl = unit(p, s - 2)
                        act.wait_ge(pv_done, n + 2)
                        for f in range(1 if b < 4 else 2):
                            w = min(4, b + 1 - 4 * f)
                            act.wait_ge(t_done, f0 + fl + f + 1)
                            act.activation(pT[u % 2][:, f * 512:f * 512 + w * P], ps[:, 4 + (fl + f) % 2, 0:w * P],
                                           ACT.Copy).then_inc(pt_copied, 1)

            act.sem_inc(pt_copied, 2)
            for g in range(5):
                pj_evac(0, g, True)
            attend(0, STEPS_IN, True, {1: lambda: pj_evac(0, 5, True)})
            with act.Fori(0, PAIRS - 1) as p:
                attend(p, STEPS_BODY, True, {st: (lambda g=g: pj_evac(p + 1, g, False)) for st, g in PJ_AT.items()})

            def qa_copy(t):
                act.wait_ge(qa_ps, t + 1)
                if t >= 2:
                    act.wait_ge(qa_tp, t - 1)
                    act.wait_ge(qa_rope, t - 1)
                act.activation(atm[t % 2].rearrange("p h d -> p (h d)"), ps[:, 7, :], ACT.Copy).then_inc(qa_tm, 1)

            def qa_turned(t):
                act.wait_ge(qa_tp, t + 1)
                act.activation(qaT[:, :, t * P:(t + 1) * P], ps[:, 7, :].rearrange("p (j m) -> p j m", j=4), ACT.Copy).then_inc(qa_out, 1)

            filler = {3 + 2 * t: (lambda t=t: qa_copy(t)) for t in range(TT)}
            filler.update({4 + 2 * t: (lambda t=t: qa_turned(t)) for t in range(TT)})
            attend(PAIRS - 1, STEPS_BODY, False, filler)
            attend(PAIRS, STEPS_IN, True, {})
            with act.Fori(PAIRS, 2 * PAIRS - 1) as p:
                attend(p, STEPS_BODY, True, {})

            def high(kt):
                if kt == 0:
                    act.wait_ge(qc_ok, 2 * PAIRS)
                if kt == KT - 1:
                    act.wait_ge(mbc_ok, 9)
                act.activation(h_hi[kt], hT[:, kt, :], ACT.Copy).then_inc(hhi_ok, 1)

            attend(2 * PAIRS - 1, STEPS_BODY, False, {(5 + kt if kt < KT - 1 else 14): (lambda kt=kt: high(kt)) for kt in range(KT)})

            def high_w(slot, n_in):
                act.wait_ge(wo_in[slot], n_in)
                for g in range(2):
                    act.activation(w_hi[slot][g], wO[slot][g].rearrange("q t n -> q (t n)"), ACT.Copy).then_inc(whi_ok, 1)

            act.wait_ge(o_done, 2 * UNITS * PAIRS)
            high_w(0, 64)
            for n in range(0, 16, 2):
                act.wait_ge(ot_ps, n + 1)
                act.wait_ge(lg_done, 2 * UNITS * PAIRS + 2)
                act.activation(oT[:, n // 2, 0:512], ps[:, n % 8, :], ACT.Copy).then_inc(ot_act, 1)
            def gates(i, more):
                for z in range(4):
                    act.wait_ge(g_ps, 4 * i + z + 1)
                    act.wait_ge(mg_done, 4 * i + z + 1)
                    act.activation(eg[z % 2], ps[:, 4 * (z % 2):4 * (z % 2) + 2, :].rearrange("q a n -> q (a n)"), ACT.Exp,
                                   scale=-1.0).then_inc(g_exp, 1)
                    if z == 0:
                        high_w(1, 64 * i + 64)
                    if z == 2 and more:
                        high_w(0, 64 * i + 128)

            act.wait_ge(ot_ps, 16)
            with act.Fori(0, KT // 2 - 1) as i:
                gates(i, True)
            gates(KT // 2 - 1, False)
            for t in range(TT + 1):
                if t < TT:
                    act.wait_ge(x1_ok, 2 * t + 2)
                    if t >= 1:
                        act.wait_ge(sq2_ok, t)
                    act.activation(sqj, x1[:, t, :], ACT.Square, accum_out=ssq[:, t:t + 1]).then_inc(sq2_ok, 1)
                    act.wait_ge(ms2_ok, t + 1)
                    act.activation(rstd[:, t:t + 1], ssq[:, t:t + 1], ACT.Sqrt).then_inc(sqrt2_ok, 1)
                if t >= 1:
                    u = t - 1
                    act.wait_ge(h2t_ps, u + 1)
                    if u >= 2:
                        act.wait_ge(lg_ps, u - 1)
                    act.activation(h2T[u % 2].rearrange("q a n -> q (a n)"), ps[:, 4:6, :].rearrange("q a n -> q (a n)"), ACT.Copy).then_inc(h2t_ok, 1)
            act.wait_ge(g_sub, 1)
            act.activation(ex4, ex4, ACT.Exp).then_inc(g_e, 1)
            act.wait_ge(d_sub, 1)
            act.activation(ee, ee, ACT.Exp).then_inc(d_e, 1)
            act.wait_ge(used_ok, 2)
            used = act.value_load(n_used[0:1, :], min_val=1, max_val=BLOCKS)

            def xt_copy(b, z):
                act.wait_ge(xt_e, b + 1)
                act.wait_ge(up_ps, b + 2)
                act.activation(xT[z].rearrange("q a n -> q (a n)"), ps[:, 0:2, :].rearrange("q a n -> q (a n)"), ACT.Copy).then_inc(xt_c, 1)

            xt_copy(0, 0)
            with act.Fori(0, BLOCKS // AHEAD) as i:
                for q in range(AHEAD):
                    b, z = AHEAD * i + q, q % 2
                    with act.If(b < used):
                        act.wait_ge(gate_ps, b + 3)
                        act.wait_ge(hid_ok, b)
                        act.activation(sg[z], ps[:, 2, :], ACT.Exp, scale=-1.0).then_inc(gexp_e, 1)
                        act.wait_ge(ht_ps, 2 * b + 2)
                        act.wait_ge(down_ps, b + 2)
                        act.activation(hidT[z][:, 2:4, :].rearrange("q a n -> q (a n)"), ps[:, 7, 0:2 * P], ACT.Copy).then_inc(ht_ok, 1)
                        xt_copy(b + 1, 1 - z)
                    act.nop()
            for t in range(TT):
                act.wait_ge(x_in[t], 48)
                if t >= 1:
                    act.wait_ge(f_sq, t)
                act.activation(sqj, x1[:, t, :], ACT.Square, accum_out=ssq[:, t:t + 1]).then_inc(f_sq, 1)
                act.wait_ge(f_ms, t + 1)
                act.activation(rstd[:, t:t + 1], ssq[:, t:t + 1], ACT.Sqrt).then_inc(f_rt, 1)

        @block.tensor
        def _(pe):
            pe.wait_ge(consts, 5)
            for t in range(TT):
                pe.wait_ge(xn_ok, t + 1)
            for n in range(16):
                kt, half = n // 2, n % 2
                if n >= 7:
                    pe.wait_ge(xt_act if (n - 7) % 2 == 0 else xt_dve, (n - 7) // 2 + 1)
                for j in range(4):
                    t = 4 * half + j
                    m = pe.transpose(ps[:, n % 7, j * P:(j + 1) * P], xs[:, t, kt * P:(kt + 1) * P], ident[:])
                m.then_inc(xt_ps, 1)
                if n == 6:
                    pe.wait_ge(acc_ok, 4)
                    for k in range(2 * KT):
                        m = pe.matmul(ps[:, 7, k:k + 1], acc[k // KT][:, (k % KT) * P:(k % KT + 1) * P], ones[:, 0:1],
                                      start=True, stop=True)
                    m.then_inc(modp_ok, 1)
            pe.wait_ge(xt_act, 8)
            pe.wait_ge(xt_dve, 8)

            def project(t):
                if t >= 2:
                    pe.wait_ge(q_copied, 2 * (t - 1))
                for kt in range(KT):
                    pe.matmul(ps[:, t % 2, 0:P_N], hT[:, kt, t * P:(t + 1) * P], wsmall[:, kt, :],
                              start=kt == 0, stop=kt == KT - 1)
                if t == 0:
                    pe.wait_ge(wi_in[1], 16)
                for kt in range(KT):
                    m = pe.matmul(ps[:, 2 + t % 2, :], hT[:, kt, t * P:(t + 1) * P], wqi[:, kt, :],
                                  start=kt == 0, stop=kt == KT - 1)
                m.then_inc(ip_ps, 1)

            def turn(t):
                pe.wait_ge(rope_ok, t + 1)
                pe.wait_ge(q_copied, 2 * (t + 1))
                pe.wait_ge(k_spread, t + 1)
                if t >= 2:
                    pe.wait_ge(it_copied, 2 * (t - 1))
                q = qtm[t % 2].rearrange("p h d -> p (h d)")
                for j in range(4):
                    pe.transpose(ps[:, 4 + t % 2, j * P:(j + 1) * P], q[:, j * P:(j + 1) * P], ident[:])
                for j in range(4):
                    m = pe.transpose(ps[:, 6 + t % 2, j * P:(j + 1) * P], ktm[t % 2][:, j, :], ident[:])
                m.then_inc(it_ps, 1)

            pe.wait_ge(wi_in[0], 48)
            for t in range(TT + 1):
                if t < TT:
                    project(t)
                if t >= 1:
                    turn(t - 1)
            pe.wait_ge(it_copied, 2 * TT)
            for n in range(N_IU):
                blk, h = B0 + n // NH, n % NH
                w = WB[blk]
                if n >= 4:
                    pe.wait_ge(relu_ok, n - 3)
                for a in range(0, w, 512):
                    e = min(a + 512, w)
                    m = pe.matmul(ps[:, 2 * (n % 4) + a // 512, 0:e - a], qiT[:, h // 2, blk * P:(blk + 1) * P],
                                  kT[:, h % 2, a:e], start=True, stop=True)
                m.then_inc(rel_ps, 1)


            def pj_group(p, g):
                j, half = g // 2, g % 2
                if g % 2 == 0:
                    pe.wait_ge(wb_in[j], 16 * (p + 1))
                pe.wait_ge(pj_out, 6 * p + g)
                if j < 2:
                    for kt in range(KT):
                        m = pe.matmul(ps[:, 7, :], wB[j][:, kt, :], hT[:, kt, half * 512:(half + 1) * 512],
                                      start=kt == 0, stop=kt == KT - 1)
                else:
                    for a in range(4):
                        t = 4 * half + a
                        for kt in range(KT):
                            m = pe.matmul(ps[:, 7, a * P:(a + 1) * P], hT[:, kt, t * P:(t + 1) * P], wB[2][:, kt, :],
                                          start=kt == 0, stop=kt == KT - 1)
                m.then_inc(pj_ps, 1)

            def attend(p, steps, more, q, k, kq, v, ready, filler):
                for s in steps:
                    if s < UNITS or more:
                        n, b, z, u, _, _ = unit(p, s)
                        ready(p + s // UNITS, u)
                        pe.wait_ge(lg_done, n + 1)
                        for a in range(0, WB[b], 512):
                            e = min(a + 512, WB[b])
                            m = pe.matmul(ps[:, 2 * (u % 2) + a // 512, 0:e - a], q[z][0:kq, b * P:(b + 1) * P],
                                          k[z][0:kq, a:e], start=True, stop=True)
                        m.then_inc(qk_done, 1)
                    if s >= 2 and (s - 2 < UNITS or more):
                        n, b, z, u, f0, fl = unit(p, s - 2)
                        pe.wait_ge(p_done, n + 1)
                        for f in range(1 if b < 4 else 2):
                            pe.wait_ge(pt_copied, f0 + fl + f + 1)
                            for a in range(min(4, b + 1 - 4 * f)):
                                kb = 4 * f + a
                                m = pe.transpose(ps[:, 4 + (fl + f) % 2, a * P:(a + 1) * P], lg[u % 4][:, kb * P:(kb + 1) * P], ident[:])
                            m.then_inc(t_done, 1)
                    if s >= 3:
                        n, b, z, u, f0, fl = unit(p, s - 3)
                        pe.wait_ge(pt_copied, f0 + fl + (1 if b < 4 else 2) + 2)
                        pe.wait_ge(o_done, n)
                        for kb in range(b + 1):
                            m = pe.matmul(ps[:, 6, 0:P], pT[u % 2][:, kb * P:(kb + 1) * P], v(p, kb), start=kb == 0, stop=kb == b)
                        m.then_inc(pv_done, 1)
                    if s in filler:
                        filler[s]()

            def ready_b(p, u):
                if u % TT == 0:
                    z = u // TT
                    pe.wait_ge(aug_ok, 4 * p + 2 + 2 * z)
                    pe.wait_ge(row_in[z], 32 * (p + 1))
                if u == 3:
                    pe.wait_ge(pj_out, 6 * p + 6)

            def v_b(p, kb):
                return vall[:, ds(p, 1), kb, :].rearrange("q o d -> q (o d)")

            pe.wait_ge(f_pre, 1)
            pe.wait_ge(relu_ok, N_IU - 3)
            pe.matmul(ps[:, 0, 0:TT * NH], upper[:], fl.rearrange("p a b -> p (a b)"), start=True, stop=False)
            pe.matmul(ps[:, 0, 0:TT * NH], ones[:], fx.rearrange("p a b -> p (a b)"), start=False, stop=True).then_inc(cum_ps, 1)
            pe.wait_ge(relu_ok, N_IU)
            pe.sem_inc(pv_done, 3)
            pj_group(0, 0)
            pe.wait_ge(cum_sb, 1)
            for t in range(TT):
                m = pe.transpose(ps[0:NH, 2 + t // 4, (t % 4) * P:(t % 4 + 1) * P], cum[:, t, :], ident[:])
            m.then_inc(cumt_ps, 1)
            for g in range(1, 5):
                pj_group(0, g)
            forget = (aq, ak, HD + 2, v_b, ready_b)
            attend(0, STEPS_IN, True, *forget, {1: lambda: pj_group(0, 5)})
            with pe.Fori(0, PAIRS - 1) as p:
                attend(p, STEPS_BODY, True, *forget, {st: (lambda g=g: pj_group(p + 1, g)) for st, g in PJ_AT.items()})

            def qa_tile(t):
                if t == 0:
                    pe.wait_ge(wqa_in, 16)
                    pe.wait_ge(pj_out, 6 * PAIRS)
                else:
                    pe.wait_ge(qa_out, t)
                for kt in range(KT):
                    m = pe.matmul(ps[:, 7, :], hT[:, kt, t * P:(t + 1) * P], wqa[:, kt, :], start=kt == 0, stop=kt == KT - 1)
                m.then_inc(qa_ps, 1)

            def qa_turn(t):
                pe.wait_ge(qa_rope, t + 1)
                for j in range(4):
                    m = pe.transpose(ps[:, 7, j * P:(j + 1) * P], atm[t % 2].rearrange("p h d -> p (h d)")[:, j * P:(j + 1) * P], ident[:])
                m.then_inc(qa_tp, 1)

            filler = {3 + 2 * t: (lambda t=t: qa_tile(t)) for t in range(TT)}
            filler.update({4 + 2 * t: (lambda t=t: qa_turn(t)) for t in range(TT)})
            attend(PAIRS - 1, STEPS_BODY, False, *forget, filler)

            def ready_a(p, u):
                if u % TT == 0:
                    pe.wait_ge(qc_ok, 2 * (p - PAIRS) + 1 + u // TT)

            def v_a(p, kb):
                return va[:, kb].rearrange("q z d -> q (z d)")

            sparse = (qcur, [kT[:, 2, :], kT[:, 3, :]], P, v_a, ready_a)
            attend(PAIRS, STEPS_IN, True, *sparse, {})
            with pe.Fori(PAIRS, 2 * PAIRS - 1) as p:
                attend(p, STEPS_BODY, True, *sparse, {})

            def modulate(n):
                if n == 0:
                    pe.wait_ge(acc_ok, 12)
                    pe.wait_ge(qa_out, TT)
                else:
                    pe.wait_ge(mbc_ok, n)
                pe.matmul(ps[:, 7, :], ones[:], acc[2 + n // 2][:, (n % 2) * 512:(n % 2 + 1) * 512], start=True, stop=True).then_inc(mbc_ps, 1)

            attend(2 * PAIRS - 1, STEPS_BODY, False, *sparse, {3 + n: (lambda n=n: modulate(n)) for n in range(8)})
            pe.wait_ge(mbc_ok, 9)

            pe.wait_ge(o_done, 2 * UNITS * PAIRS)
            for n in range(16):
                j, half = n // 2, n % 2
                src = (oa, ob)[j // 4]
                if n >= 8:
                    pe.wait_ge(ot_act if n % 2 == 0 else ot_dve, (n - 8) // 2 + 1)
                for a in range(4):
                    m = pe.transpose(ps[:, n % 8, a * P:(a + 1) * P], src[:, 4 * half + a, (j % 4) * P:(j % 4 + 1) * P], ident[:])
                m.then_inc(ot_ps, 1)
            pe.wait_ge(ot_act, 8)
            pe.wait_ge(ot_dve, 8)
            pe.wait_ge(hlo_ok, KT)
            with pe.Fori(0, KT // 2) as i:
                for z in range(4):
                    slot, half = z // 2, z % 2
                    w = wO[slot]
                    if half == 0:
                        pe.wait_ge(wo_in[slot], 64 * i + 64)
                    pe.wait_ge(mg_done, 4 * i + z + 1)
                    tok = slice(half * 512, (half + 1) * 512)
                    if half == 0:
                        pe.wait_ge(wlo_ok, 4 * i + z + 2)
                    for g in range(2):
                        for kt in range(KT):
                            rows = slice(kt * P, (kt + 1) * P)
                            w_h, h_h = w_hi[slot][g][:, rows], h_hi[kt][:, tok]
                            for k, (a, b) in enumerate(((w_h, h_h), (w_h, h_lo[kt][:, tok]), (w_lo[slot][g][:, rows], h_h))):
                                m = pe.matmul(ps[:, 4 * half + g, :], a, b,
                                              start=kt == 0 and k == 0, stop=kt == KT - 1 and k == 2)
                    m.then_inc(g_ps, 1)
                    for g in range(2):
                        for kt in range(4):
                            m = pe.matmul(ps[:, 4 * half + 2 + g, :], w[2 + g][:, kt, :], oT[:, 4 * g + kt, tok], start=kt == 0, stop=kt == 3)
                    m.then_inc(yab_ps, 1)
            for t in range(TT + 2):
                if t < TT:
                    if t % 4 == 0:
                        pe.wait_ge(mg_done, 2 * KT + 1 + t // 4)
                    for n in range(2):
                        if t >= 2:
                            pe.wait_ge(yt_ok, 2 * (t - 2) + n + 1)
                        for kt in range(KT):
                            if t == 0 and n == 0 and kt % 2 == 0:
                                pe.wait_ge(wout_in[kt // 2], 16)
                            m = pe.matmul(ps[:, 2 * (t % 2) + n, :], mT[:, kt, t * P:(t + 1) * P], wout[:, kt, n * 512:(n + 1) * 512], start=kt == 0, stop=kt == KT - 1)
                        m.then_inc(y_ps, 1)
                if 1 <= t <= TT:
                    u = t - 1
                    pe.wait_ge(h2_ok, u + 1)
                    if u >= 1:
                        pe.wait_ge(h2t_ok, u)
                    for kt in range(KT):
                        m = pe.transpose(ps[:, 4 + kt // 4, (kt % 4) * P:(kt % 4 + 1) * P], h2[u % 2][:, kt * P:(kt + 1) * P], ident[:])
                    m.then_inc(h2t_ps, 1)
                if t >= 2:
                    u = t - 2
                    if u == 0:
                        pe.wait_ge(r_in, 64)
                    pe.wait_ge(h2t_ok, u + 1)
                    if u >= 1:
                        pe.wait_ge(lg_ok, u)
                    for kt in range(KT):
                        m = pe.matmul(ps[:, 6, 0:NG + NE], h2T[u % 2][:, kt, :], wgr[:, kt, :], start=kt == 0, stop=kt == KT - 1)
                    m.then_inc(lg_ps, 1)
            pe.wait_ge(m_ok, 1)
            pe.wait_ge(dc_ok, 1)
            mxf = mx.rearrange("q t e -> q (t e)")
            pe.matmul(ps[:, 0, 0:TT * NE], strict, mb.rearrange("q t e -> q (t e)"), start=True, stop=False)
            pe.matmul(ps[:, 0, 0:TT * NE], oneb, mxf[:, 0:TT * NE], start=False, stop=True)
            pe.matmul(ps[:, 1, 0:NE], oneb, mxf[:, TT * NE:], start=True, stop=True).then_inc(rank_ps, 1)
            pe.sem_inc(gate_ps, 1)
            pe.wait_ge(used_ok, 2)
            used = pe.value_load(n_used[0:1, :], min_val=1, max_val=BLOCKS)

            def turn_rows(z, tiles):
                rows_kt = xg[z].rearrange("r (q t) -> r t q", t=KT)
                for kt in tiles:
                    m = pe.transpose(ps[:, kt // 4, (kt % 4) * P:(kt % 4 + 1) * P], rows_kt[:, kt, :], ident[:])
                return m

            pe.wait_ge(xg_in[0], 16)
            for read, more in ((gate_ps, 1), (up_ps, 2), (down_ps, 2)):
                pe.sem_inc(read, more)
            turn_rows(0, range(KT)).then_inc(xt_e, 1)
            with pe.Fori(0, BLOCKS // AHEAD) as i:
                for q in range(AHEAD):
                    b, z = AHEAD * i + q, q % 2
                    with pe.If(b < used):
                        r = pe.value_load(run_of[0:1, ds(b, 1)], min_val=0, max_val=NE - 1)
                        set_at = (r % 2) * SET + 8 * U

                        def weights_in(j):
                            pe.wait_ge(wE_in[0][j], (r // 2) * 16 + 16)
                            pe.wait_ge(wE_in[1][j], ((r + 1) // 2) * 16)

                        pe.wait_ge(xt_c, b + 1)
                        for j, ok in enumerate((gate_ps, up_ps)):
                            weights_in(j)
                            pe.wait_ge(hid_ok, b)
                            for kt in range(KT):
                                m = pe.matmul(ps[:, 2 + j, :], xT[z][:, kt, :], arena[:, ds(set_at + (4 * j * U + kt * FE), FE)],
                                              start=kt == 0, stop=kt == KT - 1)
                            m.then_inc(ok, 1)
                        pe.wait_ge(xg_in[1 - z], 32 * i + 16 * ((q + 1) // 2 + 1))
                        turn_rows(1 - z, range(5))
                        pe.wait_ge(hid_ok, b + 1)
                        hid_kt = hid[z].rearrange("r (q t) -> r t q", t=4)
                        for half in range(2):
                            for kt in range(2):
                                m = pe.transpose(ps[:, 4 + 3 * half, kt * P:(kt + 1) * P], hid_kt[:, 2 * half + kt, :], ident[:])
                            m.then_inc(ht_ps, 1)
                        turn_rows(1 - z, range(5, KT)).then_inc(xt_e, 1)
                        weights_in(2)
                        pe.wait_ge(ht_ok, 2 * b + 2)
                        pe.wait_ge(ye_ok, b)
                        for n in range(2):
                            for kt in range(4):
                                m = pe.matmul(ps[:, 5 + n, :], hidT[z][:, kt, :], arena[:, ds(set_at + (8 * U + kt * D + n * 512), 512)],
                                              start=kt == 0, stop=kt == 3)
                        m.then_inc(down_ps, 1)
                    pe.nop()

        @block.vector
        def _(dve):
            chain = Tally(dve_chain)

            def link(ins):
                dve.wait_ge(dve_chain, chain.up(ins))

            dve.wait_ge(c_in, 80)
            link(dve.tensor_copy(pos, posi))
            dve.wait_ge(freq_ok, HALF)
            for t in range(TT):
                chain.up(dve.tensor_scalar(ang[:, t, :], invf, pos[:, t:t + 1], None, ALU.mult))
            dve.wait_ge(dve_chain, chain.now())
            magic = float(1.5 * 2 ** 23)
            link(dve.tensor_scalar(angk, ang, float(1 / (2 * np.pi)), magic, ALU.mult, ALU.add))
            link(dve.tensor_scalar(angk, angk, -magic, None, ALU.add))
            p1 = 6.28125
            p2 = float(np.float32(np.round((2 * np.pi - p1) * 2 ** 19) / 2 ** 19))
            p3 = float(2 * np.pi - p1 - p2)
            link(dve.scalar_tensor_tensor(angr, angk, -p1, ang, ALU.mult, ALU.add))
            link(dve.scalar_tensor_tensor(angr, angk, -p2, angr, ALU.mult, ALU.add))
            link(dve.scalar_tensor_tensor(angr, angk, -p3, angr, ALU.mult, ALU.add))
            pi = float(np.nextafter(np.float32(np.pi), np.float32(0)))
            dve.tensor_scalar(angr, angr, pi, -pi, ALU.min, ALU.max).then_inc(ang_ok, 1)
            dve.wait_ge(silu_e, 1)
            link(dve.tensor_scalar(sil, sil, 1.0, None, ALU.add))
            link(dve.reciprocal(sil, sil))
            link(dve.tensor_tensor(sil, sil, cT, ALU.mult))

            def mod_sums(n):
                w = wslot[n % 2] if n < 4 else mod2[n % 2]
                dve.wait_ge(mod_in[n % 2] if n < 4 else mod_in[2 + n % 2], 16 * (n // 2 + 1 if n < 4 else (n - 4) // 2 + 1))
                a = acc[n // 2][:, (n % 2) * 512:(n % 2 + 1) * 512]
                link(dve.tensor_scalar(a, w[:, 0, :], sil[:, 0:1], None, ALU.mult))
                for t in range(1, KT):
                    m = dve.scalar_tensor_tensor(a, w[:, t, :], sil[:, t:t + 1], a, ALU.mult, ALU.add)
                    if t < KT - 1:
                        link(m)
                m.then_inc(acc_ok, 1)

            mod_sums(0)
            mod_sums(1)
            dve.wait_ge(ssq_ok, TT)
            dve.tensor_scalar(ssq, ssq, 1.0 / D, EPS, ALU.mult, ALU.add).then_inc(ms_ok, 1)
            dve.wait_ge(sqrt_ok, 1)
            link(dve.reciprocal(rstd, rstd))
            for t in range(TT):
                dve.tensor_scalar(xs[:, t, :], xs[:, t, :], rstd[:, t:t + 1], None, ALU.mult).then_inc(xn_ok, 1)
            mod_sums(2)
            mod_sums(3)

            dve.wait_ge(modp_ok, 1)
            dve.tensor_tensor(sh1, ps[:, 7, 0:KT], bmod[:, 0:KT], ALU.add).then_inc(mod1_ok, 1)
            link(dve.tensor_tensor(a1, ps[:, 7, KT:2 * KT], bmod[:, KT:2 * KT], ALU.add))
            dve.scalar_tensor_tensor(a1, a1, 1.0, gmix, ALU.add, ALU.mult).then_inc(mod1_ok, 1)
            dve.wait_ge(sin_ok, 2)
            link(dve.tensor_tensor(cos2[:, :, 1, :], cos2[:, :, 0, :], cos2[:, :, 0, :], ALU.mult))
            chain.up(dve.tensor_scalar(cos2[:, :, 0, :], cos2[:, :, 1, :], -2.0, 1.0, ALU.mult, ALU.add))
            link(dve.tensor_scalar(sin2[:, :, 1, :], sin2[:, :, 0, :], -1.0, None, ALU.mult))
            link(dve.tensor_copy(cos2[:, :, 1, :], cos2[:, :, 0, :]))
            dve.wait_ge(mod1_ok, 2)
            for n in range(1, 16, 2):
                dve.wait_ge(xt_ps, n + 1)
                kt, half = n // 2, n % 2
                dve.tensor_scalar(hT[:, kt, half * 512:(half + 1) * 512], ps[:, n % 7, :], a1[:, kt:kt + 1],
                                  sh1[:, kt:kt + 1], ALU.mult, ALU.add).then_inc(xt_dve, 1)

            for t in range(TT):
                dve.wait_ge(q_copied, 2 * (t + 1))
                if t >= 2:
                    dve.wait_ge(it_ps, t - 1)
                tq, tk = rt[t % 2], rk[t % 2]
                q = qtm[t % 2][:, :, 0:ROPE]
                k = kraw[t % 2][:, 0:2 * P_KA].rearrange("p (j d) -> p j d", j=2)[:, :, 0:ROPE]
                cs = cos2[:, t].rearrange("p a b -> p (a b)").unsqueeze(1)
                sn = sin2[:, t].rearrange("p a b -> p (a b)").unsqueeze(1)
                chain.up(dve.tensor_tensor(tq[:, 0], q, cs.to_broadcast([P, NH, ROPE]), ALU.mult))
                chain.up(dve.tensor_tensor(tq[:, 1], q, sn.to_broadcast([P, NH, ROPE]), ALU.mult))
                chain.up(dve.tensor_tensor(tk[:, 0], k, cs.to_broadcast([P, 2, ROPE]), ALU.mult))
                link(dve.tensor_tensor(tk[:, 1], k, sn.to_broadcast([P, 2, ROPE]), ALU.mult))
                chain.up(dve.tensor_tensor(qtm[t % 2][:, :, 0:HALF], tq[:, 0, :, 0:HALF], tq[:, 1, :, HALF:ROPE], ALU.add))
                chain.up(dve.tensor_tensor(qtm[t % 2][:, :, HALF:ROPE], tq[:, 0, :, HALF:ROPE], tq[:, 1, :, 0:HALF], ALU.add))
                kk = ktm[t % 2].rearrange("p (j z) m -> p j (z m)", j=2)
                for z in range(2):
                    o = z * (P + HD)
                    chain.up(dve.tensor_tensor(kk[:, :, o:o + HALF], tk[:, 0, :, 0:HALF], tk[:, 1, :, HALF:ROPE], ALU.add))
                    m = dve.tensor_tensor(kk[:, :, o + HALF:o + ROPE], tk[:, 0, :, HALF:ROPE], tk[:, 1, :, 0:HALF], ALU.add)
                    if z == 0:
                        chain.up(m)
                m.then_inc(rope_ok, 1)
                mod_sums(4 + t)
            dve.wait_ge(k_spread, TT)
            dve.scalar_tensor_tensor(fe, fall, -1.0, fall, ALU.mult, ALU.max).then_inc(f_ready, 1)
            dve.wait_ge(f_ln, 1)
            link(dve.scalar_tensor_tensor(fl, fall, 0.0, fe, ALU.min, ALU.subtract))
            chain.up(dve.memset(fx[:, 0, :], 0.0))
            link(dve.tensor_copy(fx[:, 1, :], fl[:, 0, :]))
            for t in range(2, TT):
                m = dve.tensor_tensor(fx[:, t, :], fx[:, t - 1, :], fl[:, t - 1, :], ALU.add)
                if t < TT - 1:
                    link(m)
            m.then_inc(f_pre, 1)
            for n in range(N_IU):
                blk, h = B0 + n // NH, n % NH
                w = WB[blk]
                s_blk = sc[:, MOFF[blk]:MOFF[blk] + w]
                dve.wait_ge(relu_ok, n + 1)
                if h == 0:
                    dve.tensor_scalar(s_blk, relu[n % 2][:, 0:w], wi[:, blk, h:h + 1], None, ALU.mult).then_inc(score_ok, 1)
                else:
                    dve.wait_ge(score_ok, n)
                    dve.scalar_tensor_tensor(s_blk, relu[n % 2][:, 0:w], wi[:, blk, h:h + 1], s_blk, ALU.mult, ALU.add).then_inc(score_ok, 1)
            dve.wait_ge(score_ok, N_IU)
            for blk in range(B0, TT):
                chain.up(dve.memset(sc[0:CHUNK, MOFF[blk] + WB[blk] - CHUNK:MOFF[blk] + WB[blk]], NEG))
            dve.wait_ge(dve_chain, chain.now())
            dve.wait_ge(cum_ps, 1)
            dve.tensor_copy(cum.rearrange("p a b -> p (a b)"), ps[:, 0, 0:TT * NH]).then_inc(cum_sb, 1)
            dve.wait_ge(cumt_ps, 1)
            cps = ps[0:NH, 2:4, :].rearrange("p a b -> p (a b)")
            dve.tensor_copy(cumT[0:NH, 0, :], cps).then_inc(cumt_sb, 1)
            dve.tensor_scalar(cumT[0:NH, 1, :], cps, -1.0, None, ALU.mult).then_inc(cumt_sb, 1)
            dve.wait_ge(cumt_sb, 2)
            dve.sem_inc(lg_done, 2)

            scb = [sc[:, MOFF[b]:MOFF[b] + WB[b]] for b in range(B0, TT)]

            def count_block(op, thr, b):
                if b >= 2:
                    dve.wait_ge(dve_chain, chain.now() - 1)
                chain.up(dve.tensor_scalar(junk[b % 2][:, 0:WB[B0 + b]], scb[b], thr(b), None, op, ALU.add,
                                           accum_out=cnt[:, b:b + 1]))

            def count(op, thr):
                for b in range(NSB):
                    count_block(op, thr, b)
                dve.wait_ge(dve_chain, chain.now())

            dve.wait_ge(zero_ok, NSB)
            dve.wait_ge(acc_ok, 12)
            count(ALU.is_ge, lambda b: 0.0)
            link(dve.tensor_scalar(cnt, cnt, float(TOPK), None, ALU.is_ge))
            chain.up(dve.tensor_scalar(sigma, cnt, 2.0, -1.0, ALU.mult, ALU.add))
            link(dve.tensor_scalar(kneed, wm, -1.0, float(TOPK), ALU.mult, ALU.add))
            link(dve.tensor_tensor(kneed, kneed, cnt, ALU.mult))
            link(dve.tensor_tensor(kneed, kneed, wm, ALU.add))
            for b in range(NSB):
                chain.up(dve.tensor_scalar(scb[b], scb[b], sigma[:, b:b + 1], None, ALU.mult))
            chain.up(dve.memset(thr_bits.bitcast(I32), 0))
            link(dve.memset(bitt.bitcast(I32), 1 << 30))

            def bit_set():
                link(dve.tensor_tensor(cand.bitcast(I32), thr_bits.bitcast(I32), bitt.bitcast(I32).to_broadcast([P, NSB]), ALU.bitwise_or))
                chain.up(dve.tensor_scalar(bitt.bitcast(I32), bitt.bitcast(I32), 1, None, ALU.logical_shift_right))

            def bit_count(b):
                count_block(ALU.is_ge, lambda b: cand[:, b:b + 1], b)

            def bit_keep():
                dve.wait_ge(dve_chain, chain.now())
                link(dve.tensor_tensor(cnt.bitcast(I32), cnt, kneed, ALU.is_ge))
                dve.sem_inc(stand, 1)
                link(dve.copy_predicated(thr_bits, cnt.bitcast(I32), cand))

            def attend(p, steps, more, bias, scale, out, col, parts):
                for s in steps:
                    if s < UNITS or more:
                        n, b, z, u, _, _ = unit(p, s)
                        w = WB[b]
                        dve.wait_ge(qk_done, n + 1)
                        dve.wait_ge(pv_done, n)
                        dve.sem_inc(stand, 1)
                        dve.tensor_tensor_reduce(lg[u % 4][:, 0:w], ps[:, 2 * (u % 2):2 * (u % 2) + 2, :].rearrange("p a n -> p (a n)")[:, 0:w],
                                                 bias(b), -scale, 3e38, ALU.add, ALU.min, nmax[:, u:u + 1]).then_inc(lg_done, 1)
                    if s >= 3:
                        n, b, z, u, _, _ = unit(p, s - 3)
                        dve.wait_ge(pv_done, n + 4)
                        link(dve.reciprocal(rinv[:, u:u + 1], rs[:, u:u + 1]))
                        dve.tensor_scalar(out[:, b, ds(col + z * HD, HD)], ps[:, 6, z * HD:(z + 1) * HD],
                                          rinv[:, u:u + 1], None, ALU.mult).then_inc(o_done, 1)
                    for part in parts.get(s, ()):
                        part()

            dve.wait_ge(win_ok, 1 + B0)

            def bias_b(b):
                return window[:, S - WB[b]:S]

            def bias_a(b):
                return sc[:, MOFF[b]:MOFF[b] + WB[b]]

            dve.wait_ge(aug1_ok, 4)
            for z in range(2):
                for j, dst in enumerate((aq, ak)):
                    dve.wait_ge(pj_out, 2 * j + 2)
                    dve.tensor_copy(dst[z][0:HD, :], raw[j][z * HD:(z + 1) * HD, :]).then_inc(aug_ok, 1)
            search = ([bit_set] + [lambda b=b: bit_count(b) for b in range(NSB)] + [bit_keep]) * BIT_STEPS
            cost = ([2] + [B0 + b + 3 for b in range(NSB)] + [4]) * BIT_STEPS
            room, parts, k, at_cost, at_room = {}, {}, 0, 0, 0
            for s in STEPS_BODY:
                room[s] = sum((s - d) % TT for d in (0, 2, 3)) + 40 * (s in PJ_AT)
            for s in STEPS_BODY:
                at_room += room[s]
                while k < len(search) and (at_cost + cost[k] / 2) * sum(room.values()) <= at_room * sum(cost):
                    at_cost += cost[k]
                    parts.setdefault(s, []).append(search[k])
                    k += 1
            assert k == len(search)
            attend(0, STEPS_IN, True, bias_b, 1.0, ob, 0, {})
            with dve.Fori(0, PAIRS - 1) as p:
                chain.enter(p, BIT_STEPS * (NSB + 4) + UNITS)
                attend(p, STEPS_BODY, True, bias_b, 1.0, ob, 2 * HD * p, parts)
                chain.leave(PAIRS - 1)

            def signs_back():
                link(dve.tensor_tensor(thr_bits, thr_bits, sigma, ALU.mult))
                for b in range(NSB):
                    chain.up(dve.tensor_scalar(scb[b], scb[b], sigma[:, b:b + 1], None, ALU.mult))
                dve.wait_ge(dve_chain, chain.now())

            def count_above():
                count(ALU.is_gt, lambda b: thr_bits[:, b:b + 1])
                link(dve.tensor_scalar(cnt, cnt, -1.0, float(TOPK), ALU.mult, ALU.add))

            def choose(b):
                w, thr = WB[B0 + b], thr_bits[:, b:b + 1]
                link(dve.tensor_scalar(eqt[:, 0:w], scb[b], thr, None, ALU.is_equal))
                link(dve.tensor_tensor_scan(pre[:, 0:w], eqt[:, 0:w], eqt[:, 0:w], 0.0, ALU.add, ALU.bypass))
                link(dve.scalar_tensor_tensor(selt[:, 0:w], pre[:, 0:w], cnt[:, b:b + 1], eqt[:, 0:w], ALU.is_le, ALU.mult))
                link(dve.scalar_tensor_tensor(selt[:, 0:w], scb[b], thr, selt[:, 0:w], ALU.is_gt, ALU.add))
                link(dve.tensor_scalar(scb[b], selt[:, 0:w], -1.0, -NEG, ALU.add, ALU.mult))

            def rope_a(t):
                dve.wait_ge(qa_tm, t + 1)
                tq = art[t % 2]
                q = atm[t % 2][:, :, 0:ROPE]
                cs = cos2[:, t].rearrange("p a b -> p (a b)").unsqueeze(1)
                sn = sin2[:, t].rearrange("p a b -> p (a b)").unsqueeze(1)
                chain.up(dve.tensor_tensor(tq[:, 0], q, cs.to_broadcast([P, NH, ROPE]), ALU.mult))
                link(dve.tensor_tensor(tq[:, 1], q, sn.to_broadcast([P, NH, ROPE]), ALU.mult))
                chain.up(dve.tensor_tensor(atm[t % 2][:, :, 0:HALF], tq[:, 0, :, 0:HALF], tq[:, 1, :, HALF:ROPE], ALU.add))
                dve.tensor_tensor(atm[t % 2][:, :, HALF:ROPE], tq[:, 0, :, HALF:ROPE], tq[:, 1, :, 0:HALF], ALU.add).then_inc(qa_rope, 1)

            work = [[signs_back], [count_above]] + [[lambda b=b: choose(b)] for b in range(NSB - 1, 1, -1)] + [[lambda: choose(1), lambda: choose(0)], []]
            parts = {3 + 2 * t: work[t] + [lambda t=t: rope_a(t)] for t in range(TT)}
            attend(PAIRS - 1, STEPS_BODY, False, bias_b, 1.0, ob, 2 * HD * (PAIRS - 1), parts)
            dve.wait_ge(dve_chain, chain.now())
            dve.wait_ge(qa_out, TT)
            for z in range(2):
                dve.tensor_copy(qcur[z], qaT[:, 0, :]).then_inc(qc_ok, 1)
            root = float(HD ** -0.5)
            attend(PAIRS, STEPS_IN, True, bias_a, root, oa, 0, {})
            with dve.Fori(0, PAIRS - 1) as p:
                chain.enter(p, UNITS)
                attend(PAIRS + p, STEPS_BODY, True, bias_a, root, oa, 2 * HD * p, {})
                chain.leave(PAIRS - 1)

            def modulate(n):
                if n == 0:
                    dve.wait_ge(bmb_in, 80)
                half = slice((n % 2) * 512, (n % 2 + 1) * 512)
                dve.wait_ge(mbc_ps, n + 1)
                dve.tensor_tensor(acc[2 + n // 2][:, half], ps[:, 7, :], bmb[:, n // 2, half], ALU.add).then_inc(mbc_ok, 1)

            def modulate_a2():
                dve.wait_ge(mbc_ok, 8)
                dve.scalar_tensor_tensor(a2, a2, 1.0, gffn, ALU.add, ALU.mult).then_inc(mbc_ok, 1)

            parts = {3 + n: [lambda n=n: modulate(n)] for n in range(8)}
            parts[11] = [modulate_a2]

            def low(kt):
                dve.wait_ge(hhi_ok, kt + 1)
                dve.tensor_tensor(h_lo[kt], hT[:, kt, :], h_hi[kt].bitcast(F32), ALU.subtract).then_inc(hlo_ok, 1)

            for kt in range(KT):
                parts.setdefault(6 + kt if kt < KT - 1 else 15, []).append(lambda kt=kt: low(kt))
            attend(2 * PAIRS - 1, STEPS_BODY, False, bias_a, root, oa, 2 * HD * (PAIRS - 1), parts)

            def low_w(slot, n):
                for g in range(2):
                    dve.wait_ge(whi_ok, n + g + 1)
                    dve.tensor_tensor(w_lo[slot][g], wO[slot][g].rearrange("q t n -> q (t n)"), w_hi[slot][g].bitcast(F32), ALU.subtract).then_inc(wlo_ok, 1)

            low_w(0, 0)
            for n in range(1, 16, 2):
                dve.wait_ge(ot_ps, n + 1)
                dve.tensor_copy(oT[:, n // 2, 512:1024], ps[:, n % 8, :]).then_inc(ot_dve, 1)
            dve.wait_ge(ot_act, 8)
            dve.sem_inc(mg_done, 2)
            def merge(i, more):
                for z in range(4):
                    dve.wait_ge(g_exp, 4 * i + z + 1)
                    e = eg[z % 2]
                    link(dve.tensor_scalar(e, e, 1.0, None, ALU.add))
                    link(dve.reciprocal(e, e))
                    dve.wait_ge(yab_ps, 4 * i + z + 1)
                    for g in range(2):
                        chain.up(dve.tensor_tensor(e[:, g * 512:(g + 1) * 512], e[:, g * 512:(g + 1) * 512],
                                                   ps[:, 4 * (z % 2) + 2 + g, :], ALU.mult))
                    dve.wait_ge(dve_chain, chain.now())
                    dve.tensor_tensor(mT[:, ds(2 * i + z // 2, 1), (z % 2) * 512:(z % 2 + 1) * 512].rearrange("q a n -> q (a n)"),
                                      e[:, 0:512], e[:, 512:1024], ALU.add).then_inc(mg_done, 1)
                    if z == 0:
                        low_w(1, 4 * i + 2)
                    if z == 2 and more:
                        low_w(0, 4 * i + 4)

            with dve.Fori(0, KT // 2 - 1) as i:
                chain.enter(i, 4 * 4)
                merge(i, True)
                chain.leave(KT // 2 - 1)
            merge(KT // 2 - 1, False)
            dve.wait_ge(r_in, 64)

            def route_in(u):
                dve.wait_ge(lg_ps, u + 1)
                dve.tensor_tensor(lgt[:, u, :], ps[:, 6, 0:NG + NE], bgr, ALU.add).then_inc(lg_ok, 1)

            for t in range(TT):
                for n in range(2):
                    cols = slice(n * 512, (n + 1) * 512)
                    dve.wait_ge(y_ps, 2 * t + n + 1)
                    if t >= 2:
                        dve.wait_ge(x1_ok, 2 * (t - 2) + n + 1)
                    dve.tensor_tensor(ytmp[t % 2][:, cols], ps[:, 2 * (t % 2) + n, :], gt1[:, cols], ALU.mult).then_inc(yt_ok, 1)
                    if n == 0:
                        dve.wait_ge(x_in[t], 32)
                    dve.wait_ge(yt_ok, 2 * t + n + 1)
                    dve.tensor_tensor(x1[:, t, cols], x1[:, t, cols], ytmp[t % 2][:, cols], ALU.add).then_inc(x1_ok, 1)
                dve.wait_ge(sq2_ok, t + 1)
                dve.tensor_scalar(ssq[:, t:t + 1], ssq[:, t:t + 1], 1.0 / D, EPS, ALU.mult, ALU.add).then_inc(ms2_ok, 1)
                dve.wait_ge(sqrt2_ok, t + 1)
                link(dve.reciprocal(rstd[:, t:t + 1], rstd[:, t:t + 1]))
                if t >= 2:
                    dve.wait_ge(h2_out[t % 2], 16 * (t // 2))
                    dve.wait_ge(h2t_ps, t - 1)
                link(dve.scalar_tensor_tensor(h2[t % 2], x1[:, t, :], rstd[:, t:t + 1], a2, ALU.mult, ALU.mult))
                dve.tensor_tensor(h2[t % 2], h2[t % 2], sh2, ALU.add).then_inc(h2_ok, 1)
                if t >= 2:
                    route_in(t - 2)
            route_in(TT - 2)
            route_in(TT - 1)

            dve.wait_ge(dc_ok, 1)
            dve.wait_ge(lg_ok, TT)
            grp, exl = lgt[:, :, 0:NG], lgt[:, :, NG:NG + NE]

            def first_of_max(vals, n, top, key, iota, onehot):
                link(dve.tensor_reduce(top, vals, AX.X, ALU.max))
                link(dve.tensor_tensor(key, vals, top.unsqueeze(2).to_broadcast([P, TT, n]), ALU.is_equal))
                link(dve.scalar_tensor_tensor(key, key, -2.0 * n, iota.unsqueeze(1).to_broadcast([P, TT, n]), ALU.mult, ALU.add))
                link(dve.tensor_reduce(kmin, key, AX.X, ALU.min))
                link(dve.tensor_tensor(onehot, key, kmin.unsqueeze(2).to_broadcast([P, TT, n]), ALU.is_equal))

            first_of_max(grp, NG, gmx, key4, i4, oh4)
            dve.tensor_tensor(ex4, grp, gmx.unsqueeze(2).to_broadcast([P, TT, NG]), ALU.subtract).then_inc(g_sub, 1)
            em4 = em.rearrange("q t (g e) -> q t g e", g=NG)
            link(dve.tensor_tensor(em4, exl.rearrange("q t (g e) -> q t g e", g=NG),
                                   oh4.unsqueeze(3).to_broadcast([P, TT, NG, EPG]), ALU.mult))
            link(dve.tensor_reduce(ein, em.rearrange("q t (g e) -> q t e g", g=NG), AX.X, ALU.add))
            first_of_max(ein, EPG, v1, key8, i8, oh8[0])
            link(dve.scalar_tensor_tensor(ein, oh8[0], NEG, ein, ALU.mult, ALU.add))
            first_of_max(ein, EPG, v2, key8, i8, oh8[1])
            dve.tensor_tensor(ee, v2, v1, ALU.subtract).then_inc(d_sub, 1)
            for k in range(2):
                chain.up(dve.tensor_tensor(ohe[k].rearrange("q t (g e) -> q t g e", g=NG), oh4.unsqueeze(3).to_broadcast([P, TT, NG, EPG]),
                                           oh8[k].unsqueeze(2).to_broadcast([P, TT, NG, EPG]), ALU.mult))
            dve.wait_ge(dve_chain, chain.now())
            chain.up(dve.memset(mx[:, 0, :], 0.0))
            link(dve.tensor_tensor(mb, ohe[0], ohe[1], ALU.add))
            for t in range(TT):
                m = dve.tensor_tensor(mx[:, t + 1, :], mx[:, t, :], mb[:, t, :], ALU.add)
                if t < TT - 1:
                    link(m)
            m.then_inc(m_ok, 1)
            dve.wait_ge(g_e, 1)
            link(dve.tensor_reduce(pgr, ex4, AX.X, ALU.add))
            dve.wait_ge(d_e, 1)
            link(dve.tensor_scalar(v1, ee, 1.0, None, ALU.add))
            link(dve.tensor_tensor(pgr, pgr, v1, ALU.mult))
            link(dve.reciprocal(g12[:, 0, :], pgr))
            link(dve.tensor_tensor(g12[:, 1, :], g12[:, 0, :], ee, ALU.mult))
            chain.up(dve.tensor_copy(slt[:, :, :, 2], g12.bitcast(I32)))
            dve.wait_ge(rank_ps, 1)
            link(dve.tensor_scalar(nbi.bitcast(I32), ps[:, 1, 0:NE], float(P - 1), None, ALU.add))
            link(dve.tensor_scalar(nbi.bitcast(I32), nbi.bitcast(I32), 7, None, ALU.logical_shift_right))
            link(dve.tensor_copy(nbf, nbi.bitcast(I32)))
            link(dve.tensor_tensor_scan(pend, nbf, nbf, 0.0, ALU.add, ALU.bypass))
            link(dve.tensor_tensor(pst, pend, nbf, ALU.subtract))
            link(dve.tensor_scalar(pst, pst, float(P), None, ALU.mult))
            link(dve.tensor_tensor(em, ps[:, 0, 0:TT * NE].rearrange("q (t e) -> q t e", t=TT), pst.unsqueeze(1).to_broadcast([P, TT, NE]), ALU.add))
            for k in range(2):
                chain.up(dve.tensor_tensor(ohe[k], ohe[k], em, ALU.mult))
            dve.wait_ge(dve_chain, chain.now())
            for k in range(2):
                chain.up(dve.tensor_reduce(dstf[:, k, :], ohe[k], AX.X, ALU.add))
            dve.wait_ge(dve_chain, chain.now())
            dve.tensor_copy(dsti, dstf).then_inc(dest_ok, 1)
            link(dve.tensor_scalar(nonempty, nbf, 0.0, None, ALU.is_gt))
            link(dve.tensor_tensor_scan(runs_to, nonempty, nonempty, 0.0, ALU.add, ALU.bypass))
            link(dve.tensor_tensor(cmpr, runs_to.unsqueeze(1).to_broadcast([P, NE, NE]), ib[:, 0:NE].unsqueeze(2).to_broadcast([P, NE, NE]), ALU.is_le))
            chain.up(dve.tensor_tensor(blkr, cmpr, nbf.unsqueeze(1).to_broadcast([P, NE, NE]), ALU.mult))
            chain.up(dve.tensor_copy(n_runs, runs_to[:, NE - 1:NE]))
            link(dve.tensor_reduce(begins, cmpr, AX.X, ALU.add))
            chain.up(dve.tensor_scalar(run_e, begins, float(NE - 1), None, ALU.min))
            dve.wait_ge(dve_chain, chain.now())
            link(dve.tensor_reduce(begins, blkr, AX.X, ALU.add))
            chain.up(dve.memset(run_free[:, 0:1], 1))
            chain.up(dve.tensor_scalar(run_free[:, 1:NE], begins[:, 0:NE - 1], 2.0, None, ALU.add))
            dve.wait_ge(dve_chain, chain.now())
            dve.sem_inc(used_ok, 1)
            link(dve.tensor_tensor(cmpb, pend.unsqueeze(1).to_broadcast([P, BLOCKS, NE]), ib.unsqueeze(2).to_broadcast([P, BLOCKS, NE]), ALU.is_le))
            link(dve.tensor_tensor(cmpb, cmpb, nonempty.unsqueeze(1).to_broadcast([P, BLOCKS, NE]), ALU.mult))
            link(dve.tensor_reduce(bef, cmpb, AX.X, ALU.add))
            chain.up(dve.tensor_copy(run_of, bef))
            dve.wait_ge(dve_chain, chain.now())
            dve.tensor_copy(n_used, pend[:, NE - 1:NE]).then_inc(used_ok, 1)

            dve.wait_ge(used_ok, 2)
            used = dve.value_load(n_used[0:1, :], min_val=1, max_val=BLOCKS)
            with dve.Fori(0, BLOCKS // AHEAD) as i:
                chain.enter(i, AHEAD * 3)
                for q in range(AHEAD):
                    b, z = AHEAD * i + q, q % 2
                    with dve.If(b < used):
                        dve.wait_ge(gexp_e, b + 1)
                        link(dve.tensor_scalar(sg[z], sg[z], 1.0, None, ALU.add))
                        link(dve.reciprocal(sg[z], sg[z]))
                        link(dve.tensor_tensor(sg[z], sg[z], ps[:, 2, :], ALU.mult))
                        dve.wait_ge(up_ps, b + 3)
                        dve.wait_ge(ht_ps, 2 * b)
                        dve.tensor_tensor(hid[z], sg[z], ps[:, 3, :], ALU.mult).then_inc(hid_ok, 1)
                        dve.wait_ge(ht_ps, 2 * b + 1)
                        dve.wait_ge(down_ps, b + 2)
                        dve.tensor_copy(hidT[z][:, 0:2, :].rearrange("q a n -> q (a n)"), ps[:, 4, 0:2 * P]).then_inc(ht_ok, 1)
                        dve.wait_ge(down_ps, b + 3)
                        dve.wait_ge(idx_in[z], 32 * i + 16 * (q // 2 + 1))
                        dve.wait_ge(y_out[z], 32 * i + 16 * (q // 2))
                        dve.scalar_tensor_tensor(ye[z], ps[:, 5:7, :].rearrange("q a n -> q (a n)"), idx[q][:, 2:3].bitcast(F32), gt2,
                                                 ALU.mult, ALU.mult).then_inc(ye_ok, 1)
                    dve.nop()
                chain.leave(BLOCKS // AHEAD)
            dve.wait_ge(gf_in, 16)
            for t in range(TT):
                dve.wait_ge(f_sq, t + 1)
                dve.tensor_scalar(ssq[:, t:t + 1], ssq[:, t:t + 1], 1.0 / D, EPS, ALU.mult, ALU.add).then_inc(f_ms, 1)
                dve.wait_ge(f_rt, t + 1)
                dve.reciprocal(rstd[:, t:t + 1], rstd[:, t:t + 1]).then_inc(yt_ok, 1)
                dve.wait_ge(yt_ok, 2 * TT + t + 1)
                dve.scalar_tensor_tensor(x1[:, t, :], x1[:, t, :], rstd[:, t:t + 1], gfin, ALU.mult, ALU.mult).then_inc(f_ok, 1)


_INS = ['x', 'c', 'positions', 'w_mod', 'b_mod', 'g_mix', 'w_in', 'b_forget', 'w_out_a', 'w_out_b', 'w_out', 'g_ffn',
        'w_group', 'b_group', 'w_router', 'b_router', 'w_e_gate', 'w_e_up', 'w_e_down', 'g_final']
_OUTS = [((1, S, D), 'float32')]


def kernel(**inputs):
    import numpy as _np
    import concourse.bacc as _bacc
    from concourse import mybir as _mybir
    from concourse.bass_utils import run_bass_kernel_spmd as _run

    nc = _bacc.Bacc("TRN2", target_bir_lowering=False, num_devices=1)
    arrays, args = {}, []
    for name in _INS:
        a = _np.ascontiguousarray(inputs[name])
        arrays[f"in_{name}_dram"] = a
        args.append(nc.dram_tensor(f"in_{name}_dram", a.shape, _mybir.dt.from_np(a.dtype), kind="ExternalInput").ap())
    for i, (shape, dtype) in enumerate(_OUTS):
        dt = _mybir.dt.from_np(_np.dtype(dtype))
        args.append(nc.dram_tensor(f"out_{i}_dram", shape, dt, kind="ExternalOutput").ap())
    build(nc, *args)
    r = _run(nc, [arrays], core_ids=[0])
    got = tuple(r.results[0][f"out_{i}_dram"] for i in range(len(_OUTS)))
    return got[0]
```
